# Optimizing a Trainium2 kernel written in Bass

```python
import math
import jax, jax.numpy as jnp
from jax import lax
import numpy as np

D_MODEL = 2048
BATCH = 1
SEQ = 512
DEPTH = 1

N_HEADS_A = 8
HEAD_DIM_A = 128
D_A = N_HEADS_A * HEAD_DIM_A
MOBA_BLOCK = 256
MOBA_TOPK = 3
Q_CHUNK = 32
N_BUCKETS = 32
MAX_DISTANCE = 128
N_HEADS_B = 8
QK_DIM_B = 128
V_DIM_B = 128
D_B_QK = N_HEADS_B * QK_DIM_B
D_B = N_HEADS_B * V_DIM_B
RET_CHUNK = 128
ROT_BASE = 10000.0
D_PLE = 256
EPS = 1e-6
SPLIT_SIZES = (D_A, D_A, D_A, D_A, D_B_QK, D_B_QK, D_B, D_B, D_MODEL, D_MODEL)
D_IN = sum(SPLIT_SIZES)

kernel_name = 'hybrid_moba_retention_gated_block'

def rms_norm(x, g):
    xf = x.astype(jnp.float32)
    y = xf * lax.rsqrt(jnp.mean(xf * xf, axis=-1, keepdims=True) + EPS)
    return (y * g.astype(jnp.float32)).astype(x.dtype)

def t5_bucket(n):
    max_exact = N_BUCKETS // 2
    nf = jnp.maximum(n, 1).astype(jnp.float32)
    large = max_exact + (jnp.log(nf / max_exact) / math.log(MAX_DISTANCE / max_exact)
                         * (N_BUCKETS - max_exact)).astype(jnp.int32)
    large = jnp.minimum(large, N_BUCKETS - 1)
    return jnp.where(n < max_exact, n, large)

def moba_attention(q, k, v, rel_bias):
    B, S, H, dh = q.shape
    f32 = jnp.float32
    L = MOBA_BLOCK
    nb = -(-S // L)
    s_pad = nb * L
    pad = ((0, 0), (0, s_pad - S), (0, 0), (0, 0))
    qh = jnp.pad(q.astype(f32), pad).transpose(0, 2, 1, 3)
    kb = jnp.pad(k.astype(f32), pad).transpose(0, 2, 1, 3).reshape(B, H, nb, L, dh)
    vb = jnp.pad(v.astype(f32), pad).transpose(0, 2, 1, 3).reshape(B, H, nb, L, dh)

    k_mean = jnp.mean(kb, axis=3)
    gate = jnp.einsum('bhsd,bhnd->bhsn', qh, k_mean)
    q_blk = jnp.arange(s_pad) // L
    past = jnp.arange(nb)[None, :] < q_blk[:, None]
    gate = jnp.where(past[None, None], gate, -jnp.inf)
    n_sel = max(1, min(MOBA_TOPK, nb - 1))
    top_val, top_idx = lax.top_k(gate, n_sel)
    sel_valid = jnp.isfinite(top_val)

    scale = dh ** -0.5
    rel_bias_t = rel_bias.astype(f32).T
    bi = jnp.arange(B)[:, None, None, None]
    hi = jnp.arange(H)[None, :, None, None]
    hi5 = jnp.arange(H)[None, :, None, None, None]
    ar_q = jnp.arange(Q_CHUNK)
    ar_l = jnp.arange(L)

    def chunk(c):
        q0 = c * Q_CHUNK
        qc = lax.dynamic_slice_in_dim(qh, q0, Q_CHUNK, axis=2)
        idx = lax.dynamic_slice_in_dim(top_idx, q0, Q_CHUNK, axis=2)
        valid = lax.dynamic_slice_in_dim(sel_valid, q0, Q_CHUNK, axis=2)
        qpos = q0 + ar_q
        k_sel = kb[bi, hi, idx]
        v_sel = vb[bi, hi, idx]
        s_sel = jnp.einsum('bhqd,bhqnld->bhqnl', qc, k_sel) * scale
        kpos_sel = idx[..., None] * L + ar_l
        dist_sel = qpos[None, None, :, None, None] - kpos_sel
        s_sel = s_sel + rel_bias_t[hi5, t5_bucket(jnp.maximum(dist_sel, 0))]
        s_sel = jnp.where(valid[..., None], s_sel, -jnp.inf)
        blk = q0 // L
        k_own = lax.dynamic_index_in_dim(kb, blk, axis=2, keepdims=False)
        v_own = lax.dynamic_index_in_dim(vb, blk, axis=2, keepdims=False)
        s_own = jnp.einsum('bhqd,bhld->bhql', qc, k_own) * scale
        dist_own = qpos[:, None] - (blk * L + ar_l)[None, :]
        s_own = s_own + rel_bias_t[:, t5_bucket(jnp.maximum(dist_own, 0))][None]
        s_own = jnp.where((dist_own >= 0)[None, None], s_own, -jnp.inf)
        logits = jnp.concatenate([s_sel.reshape(B, H, Q_CHUNK, n_sel * L), s_own], axis=-1)
        probs = jax.nn.softmax(logits, axis=-1)
        p_sel = probs[..., :n_sel * L].reshape(B, H, Q_CHUNK, n_sel, L)
        p_own = probs[..., n_sel * L:]
        return (jnp.einsum('bhqnl,bhqnld->bhqd', p_sel, v_sel)
                + jnp.einsum('bhql,bhld->bhqd', p_own, v_own))

    out = lax.map(chunk, jnp.arange(s_pad // Q_CHUNK))
    out = out.transpose(1, 0, 3, 2, 4).reshape(B, s_pad, H, dh)
    return out[:, :S]

def rotate_pairs(t, cos, sin):
    t2 = t.reshape(t.shape[:-1] + (t.shape[-1] // 2, 2))
    a, b = t2[..., 0], t2[..., 1]
    return jnp.stack([a * cos - b * sin, b * cos + a * sin], axis=-1).reshape(t.shape)

def retention(q, k, v):
    B, S, H, dk = q.shape
    dv = v.shape[-1]
    f32 = jnp.float32
    C = RET_CHUNK
    N = S // C
    pos = jnp.arange(S, dtype=f32)
    theta = 1.0 / (ROT_BASE ** jnp.linspace(0.0, 1.0, dk // 2, dtype=f32))
    ang = pos[:, None] * theta[None, :]
    cos, sin = jnp.cos(ang)[:, None, :], jnp.sin(ang)[:, None, :]
    q = rotate_pairs(q.astype(f32), cos, sin)
    k = rotate_pairs(k.astype(f32), cos, sin) * (dk ** -0.5)
    log_gamma = jnp.log(1.0 - 2.0 ** (-5.0 - jnp.arange(H, dtype=f32)))

    qc = q.reshape(B, N, C, H, dk).transpose(0, 3, 1, 2, 4)
    kc = k.reshape(B, N, C, H, dk).transpose(0, 3, 1, 2, 4)
    vc = v.astype(f32).reshape(B, N, C, H, dv).transpose(0, 3, 1, 2, 4)

    i = jnp.arange(C)
    diff = i[:, None] - i[None, :]
    decay_mask = jnp.where(diff >= 0,
                           jnp.exp(jnp.maximum(diff, 0).astype(f32) * log_gamma[:, None, None]),
                           0.0)
    inner = jnp.einsum('bhncd,bhnmd->bhncm', qc, kc) * decay_mask[None, :, None]
    o_inner = jnp.einsum('bhncm,bhnme->bhnce', inner, vc)

    zeta = jnp.exp((C - 1 - i).astype(f32)[None, :] * log_gamma[:, None])
    kv = jnp.einsum('bhncd,bhnce->bhnde', kc * zeta[None, :, None, :, None], vc)
    chunk_decay = jnp.exp(C * log_gamma)[None, :, None, None]

    def step(R, kv_n):
        return R * chunk_decay + kv_n, R

    _, R_prev = lax.scan(step, jnp.zeros((B, H, dk, dv), f32), kv.transpose(2, 0, 1, 3, 4))
    xi = jnp.exp((i + 1).astype(f32)[None, :] * log_gamma[:, None])
    o_cross = jnp.einsum('bhncd,nbhde->bhnce', qc * xi[None, :, None, :, None], R_prev)
    o = (o_inner + o_cross).reshape(B, H, S, dv)
    o = o * lax.rsqrt(jnp.mean(o * o, axis=-1, keepdims=True) + EPS)
    return o.transpose(0, 2, 1, 3)

def setup_inputs(seed: int = 0) -> dict:
    key = jax.random.key(seed)
    ks = jax.random.split(key, 13)
    f32 = jnp.float32
    nrm = lambda k, shape, s: jax.random.normal(k, shape, f32) * s
    return {
        'x': nrm(ks[0], (BATCH, SEQ, D_MODEL), 1.0),
        'p': nrm(ks[1], (DEPTH, BATCH, SEQ, D_PLE), 1.0),
        'g_mix': 1.0 + nrm(ks[2], (DEPTH, D_MODEL), 0.02),
        'w_in': nrm(ks[3], (DEPTH, D_MODEL, D_IN), D_MODEL ** -0.5),
        'w_a': nrm(ks[4], (DEPTH, D_A, D_MODEL), D_A ** -0.5),
        'w_b': nrm(ks[5], (DEPTH, D_B, D_MODEL), D_B ** -0.5),
        'w_out': nrm(ks[6], (DEPTH, D_MODEL, D_MODEL), D_MODEL ** -0.5),
        'g_ple': 1.0 + nrm(ks[7], (DEPTH, D_MODEL), 0.02),
        'w_ple_gate': nrm(ks[8], (DEPTH, D_MODEL, D_MODEL), D_MODEL ** -0.5),
        'w_ple_proj': nrm(ks[9], (DEPTH, D_PLE, D_MODEL), D_PLE ** -0.5),
        'rel_bias': nrm(ks[10], (N_BUCKETS, N_HEADS_A), 0.5),
        'g_final': 1.0 + nrm(ks[11], (D_MODEL,), 0.02),
    }

def reference(x, p, g_mix, w_in, w_a, w_b, w_out, g_ple, w_ple_gate, w_ple_proj, rel_bias, g_final):
    B, S, _ = x.shape
    split_at = [int(s) for s in np.cumsum(SPLIT_SIZES)[:-1]]
    for i in range(DEPTH):
        h = rms_norm(x, g_mix[i])
        proj = h @ w_in[i]
        q_a, k_a, v_a, z_a, q_b, k_b, v_b, z_b, g_a, g_b = jnp.split(proj, split_at, axis=-1)
        y_a = moba_attention(q_a.reshape(B, S, N_HEADS_A, HEAD_DIM_A),
                             k_a.reshape(B, S, N_HEADS_A, HEAD_DIM_A),
                             v_a.reshape(B, S, N_HEADS_A, HEAD_DIM_A), rel_bias)
        y_a = y_a.reshape(B, S, D_A).astype(x.dtype) * jax.nn.silu(z_a)
        y_b = retention(q_b.reshape(B, S, N_HEADS_B, QK_DIM_B),
                        k_b.reshape(B, S, N_HEADS_B, QK_DIM_B),
                        v_b.reshape(B, S, N_HEADS_B, V_DIM_B))
        y_b = y_b.reshape(B, S, D_B).astype(x.dtype) * jax.nn.silu(z_b)
        merged = jax.nn.sigmoid(g_a) * (y_a @ w_a[i]) + jax.nn.sigmoid(g_b) * (y_b @ w_b[i])
        x = x + merged @ w_out[i]
        hp = rms_norm(x, g_ple[i])
        x = x + jax.nn.sigmoid(hp @ w_ple_gate[i]) * (p[i] @ w_ple_proj[i])
    return rms_norm(x, g_final)


_drawn_inputs = setup_inputs


def setup_inputs(seed=0):
    import zlib

    import numpy as np

    out = dict(_drawn_inputs(seed))
    spreads = {}
    factors = {'g_mix': 4.705, 'g_ple': 8.0, 'rel_bias': 3.112, 'g_final': 2.905}
    for name, (base, spread) in spreads.items():
        noise = np.random.default_rng([zlib.crc32(name.encode()), seed]).standard_normal(out[name].shape)
        drawn = base * np.exp(spread * noise) if base else spread * noise
        out[name] = __import__('jax').numpy.asarray(drawn.astype(out[name].dtype))
    for name, factor in factors.items():
        out[name] = (out[name] * factor).astype(out[name].dtype)
    return out
```

```python
from contextlib import ExitStack

import numpy as np
import concourse.bass as bass
from concourse import mybir

P = 128
S, D = 512, 2048
NH, DH = 8, 128
D_A = NH * DH
D_PLE = 256
EPS = 1e-6
BUCKETS, MAX_DISTANCE = 32, 128
BLOCK = 256
ROT_BASE = 10000.0

CH = 512
KT = D // P
KY = D_A // P
TT = S // P
NC_ = D // CH
RAW = 8
SPLIT = 4
LEAD = SPLIT - 1
GATES = 4 * D_A * 2
REV = 640
MASK = -1.0e30
BIG = 1.0e38

HEAD_STEPS = 2 * NH * KT
MERGE_STEPS = 2 * (KT + KY)
OUT0 = HEAD_STEPS + NC_ * MERGE_STEPS
PLE0 = OUT0 + NC_ * KT
GATE0 = PLE0 + NC_ * (D_PLE // P)
STEPS = GATE0 + NC_ * KT

F32, F32R = mybir.dt.float32, mybir.dt.float32r
ACT = mybir.ActivationFunctionType
ALU = mybir.AluOpType
AX = mybir.AxisListType
COPY = ACT.Copy


def shape_constants():
    f = np.float32
    dist = 511 - np.arange(REV)
    n = np.maximum(dist, 0)
    exact = BUCKETS // 2
    large = exact + (np.log(np.maximum(n, 1).astype(f) / f(exact)) / f(np.log(MAX_DISTANCE / exact))
                     * f(BUCKETS - exact)).astype(np.int32)
    bucket = np.where(n < exact, n, np.minimum(large, BUCKETS - 1))
    onehot = ((np.arange(BUCKETS)[:, None] == bucket[None]) & (dist >= 0)[None]).astype(f)
    mask = np.broadcast_to(np.where(dist >= 0, f(0), f(MASK)), (NH, REV)).astype(f)
    theta = (f(1) / (f(ROT_BASE) ** np.linspace(0, 1, DH // 2, dtype=f))).astype(f)
    ang = (np.arange(S, dtype=f)[:, None] * theta[None]).astype(f).T
    cos, sin = np.cos(ang).astype(f), np.sin(ang).astype(f)
    gamma = 1.0 - 2.0 ** (-5.0 - np.arange(NH))
    diff = np.arange(S)[None, :] - np.arange(P)[:, None]
    decay = np.where(diff >= 0, gamma[:, None, None] ** np.maximum(diff, 0), 0.0).astype(f)
    return {
        "c_onehot": onehot, "c_mask": mask,
        "c_cos": np.concatenate([cos, cos]), "c_sin": np.concatenate([sin, -sin]),
        "c_decay": decay, "c_ident": np.eye(P, dtype=f),
    }


def hybrid_block(nc, x, p, g_mix, w_in, w_a, w_b, w_out, g_ple, w_ple_gate, w_ple_proj, rel_bias,
                 g_final, c_onehot, c_mask, c_cos, c_sin, c_decay, c_ident, out):
    x2d = x.rearrange("b s d -> (b s) d")
    p2d = p.rearrange("l b s d -> (l b s) d")
    out2d = out.rearrange("b s d -> (b s) d")
    W_in = w_in.rearrange("l k n -> (l k) n")
    W_a = w_a.rearrange("l k n -> (l k) n")
    W_b = w_b.rearrange("l k n -> (l k) n")
    W_out = w_out.rearrange("l k n -> (l k) n")
    W_pg = w_ple_gate.rearrange("l k n -> (l k) n")
    W_pp = w_ple_proj.rearrange("l k n -> (l k) n")

    bias_row = nc.dram_tensor("bias_row", [NH, REV], F32)
    bias_rep = nc.dram_tensor("bias_rep", [NH * P * REV + REV], F32)

    top = [(nc.sbuf_base + 31) // 32 * 32]

    def at(name, shape, dt, offset):
        return nc.alloc_sbuf_tensor_at(name, shape, dt, offset=offset)

    def place(name, shape, dt=F32):
        offset = top[0]
        top[0] += (4 * int(np.prod(shape[1:])) + 31) // 32 * 32
        assert top[0] <= nc.sbuf_usable_end, (name, top[0])
        return at(name, shape, dt, offset), offset

    hT_hi, hT_at = place("hT_hi", [P, KT, S], F32R)
    hT_lo, _ = place("hT_lo", [P, KT, S], F32R)
    yT_hi, yT_at = place("yT_hi", [P, KT, S], F32R)
    yT_lo, _ = place("yT_lo", [P, KT, S], F32R)
    raw, _ = place("raw", [P, RAW, CH])
    w_hi, _ = place("w_hi", [P, SPLIT, CH], F32R)
    w_lo, _ = place("w_lo", [P, SPLIT, CH], F32R)
    pT_hi, _ = place("pT_hi", [P, 2, S], F32R)
    pT_lo, _ = place("pT_lo", [P, 2, S], F32R)
    ident, _ = place("ident", [P, P])
    ones, _ = place("ones", [P, P])
    gmix_col, _ = place("gmix_col", [P, KT])
    gple_col, _ = place("gple_col", [P, KT])
    eps_col, _ = place("eps_col", [P, 1])
    sq_x, _ = place("sq_x", [P, TT])
    rms_x, _ = place("rms_x", [P, TT])
    inv_x, _ = place("inv_x", [P, TT])
    sq1, _ = place("sq1", [P, TT, NC_])
    sum1, _ = place("sum1", [P, TT])
    rms1, _ = place("rms1", [P, TT])
    inv1, _ = place("inv1", [P, TT])
    half1, _ = place("half1", [P, TT])
    sq2, _ = place("sq2", [P, TT, NC_])
    sum2, _ = place("sum2", [P, TT])
    rms2, _ = place("rms2", [P, TT])
    inv2, _ = place("inv2", [P, TT])
    k_sum, _ = place("k_sum", [P, 1])
    k_mean, _ = place("k_mean", [P, 1])
    finite, _ = place("finite", [P, 2])
    cap, _ = place("cap", [P, 2])
    neg_max, _ = place("neg_max", [P, TT])
    row_sum, _ = place("row_sum", [P, TT])
    row_inv, _ = place("row_inv", [P, TT])
    region = top[0]
    KIB = 1024
    assert region + 40 * KIB <= nc.sbuf_usable_end
    x_nat = at("x_nat", [P, TT, D], F32, region)
    p_nat = at("p_nat", [P, TT, D_PLE], F32, yT_at)
    onehot = at("onehot", [BUCKETS, REV], F32, yT_at + 4 * KIB)
    mask_row = at("mask_row", [NH, REV], F32, yT_at + 7 * KIB)
    bias_vec = at("bias_vec", [NH, REV], F32, yT_at + 10 * KIB)
    rel_sb = at("rel_sb", [BUCKETS, NH], F32, yT_at + 13 * KIB)
    q_sb = at("q_sb", [P, S], F32, region)
    k_sb = at("k_sb", [P, S], F32, region + 2 * KIB)
    v_sb = at("v_sb", [P, S], F32, region + 4 * KIB)
    z_half = at("z_half", [P, S], F32, region + 6 * KIB)
    z_tanh = at("z_tanh", [P, S], F32, region + 8 * KIB)
    v_nat = at("v_nat", [P, TT, DH], F32, region + 10 * KIB)
    probs = at("probs", [P, 10 * P], F32, region + 12 * KIB)
    probsT = at("probsT", [P, TT, S], F32, region + 17 * KIB)
    rot_cos = at("rot_cos", [P, S], F32, region + 17 * KIB)
    rot_sin = at("rot_sin", [P, S], F32, region + 19 * KIB)
    o_sq = at("o_sq", [P, S], F32, region + 21 * KIB)
    o_rms = at("o_rms", [P, S], F32, region + 23 * KIB)
    table = at("table", [P, S], F32, region + 25 * KIB)
    y32 = at("y32", [P, S], F32, region + 27 * KIB)
    cos_sb = at("cos_sb", [P, S], F32, region + 29 * KIB)
    sin_sb = at("sin_sb", [P, S], F32, region + 31 * KIB)
    sq_junk = at("sq_junk", [P, D], F32, yT_at + 16 * KIB)
    o_inv = at("o_inv", [P, S], F32, region + 33 * KIB)
    merged = at("merged", [P, KT, S], F32, region)
    g_tanh = at("g_tanh", [P, 4, S], F32, region + 32 * KIB)
    x_res = at("x_res", [P, TT, D], F32, region)
    junk = at("junk", [P, CH], F32, region + 32 * KIB)
    pg_tanh = at("pg_tanh", [P, TT, CH], F32, region + 32 * KIB)
    ple = at("ple", [P, TT, D], F32, hT_at)
    gfin = at("gfin", [P, D], F32, hT_at + 32 * KIB)
    junk2 = at("junk2", [P, CH], F32, hT_at + 40 * KIB)

    with ExitStack() as ctx:
        bank = [ctx.enter_context(nc.psum_tensor(f"bank{i}", [P, CH], F32)) for i in range(8)]

        def sem(name):
            return ctx.enter_context(nc.semaphore(name))

        ident_landed, p_landed, x_landed = sem("ident_landed"), sem("p_landed"), [sem(f"x_landed{t}") for t in range(TT)]
        small_landed, rel_landed = sem("small_landed"), sem("rel_landed")
        sq_done, rms_done, inv_done, scaled = sem("sq_done"), sem("rms_done"), sem("inv_done"), sem("scaled")
        ones_set = sem("ones_set")
        bias_mm, bias_added, bias_stored, bias_spread = sem("bias_mm"), sem("bias_added"), sem("bias_stored"), sem("bias_spread")
        p_turned, p_hi, p_lo = sem("p_turned"), sem("p_hi"), sem("p_lo")
        x_turned, h_hi, h_lo = sem("x_turned"), sem("h_hi"), sem("h_lo")
        raw_landed = [sem(f"raw_landed{i}") for i in range(RAW)]
        hi_ready, lo_ready, step_done = sem("hi_ready"), sem("lo_ready"), sem("step_done")
        acc_done = sem("acc_done")
        bank_read = [sem(f"bank_read{j}") for j in range(4)]
        merge_read = [sem(f"merge_read{j}") for j in range(4)]
        v_turned, v_nat_ready = sem("v_turned"), sem("v_nat_ready")
        k_summed, k_mean_ready = sem("k_summed"), sem("k_mean_ready")
        scores_done, gate_finite, cap_ready = sem("scores_done"), sem("gate_finite"), sem("cap_ready")
        biased, max_ready, exp_done = sem("biased"), sem("max_ready"), sem("exp_done")
        inv_ready, probs_ready = sem("inv_ready"), sem("probs_ready")
        p_turn, pT_act, pT_dve = sem("p_turn"), sem("pT_act"), sem("pT_dve")
        zs_ready, table_landed, rot_landed = sem("zs_ready"), sem("table_landed"), sem("rot_landed")
        rot_cos_done, rot_sin_done, rotated = sem("rot_cos_done"), sem("rot_sin_done"), sem("rotated")
        pv_done, osq_ready, mean_done, root_ready = sem("pv_done"), sem("osq_ready"), sem("mean_done"), sem("root_ready")
        oinv_ready, gated, y_ready, y_hi, y_lo = sem("oinv_ready"), sem("gated"), sem("y_ready"), sem("y_hi"), sem("y_lo")
        merged_ready, tanh_ready = sem("merged_ready"), sem("tanh_ready")
        m_hi, m_lo = sem("m_hi"), sem("m_lo")
        xres_landed, x1_sq = sem("xres_landed"), sem("x1_sq")
        x1_turned, hp_hi, hp_lo = sem("x1_turned"), sem("hp_hi"), sem("hp_lo")
        sum1_ready, rms1_ready, inv1_ready, half1_ready = sem("sum1_ready"), sem("rms1_ready"), sem("inv1_ready"), sem("half1_ready")
        gfin_landed, pg_added, x2_ready, x2_sq = sem("gfin_landed"), sem("pg_added"), sem("x2_ready"), sem("x2_sq")
        sum2_ready, rms2_ready, inv2_ready = sem("sum2_ready"), sem("rms2_ready"), sem("inv2_ready")
        out_ready, out_stored = sem("out_ready"), sem("out_stored")

        block = ctx.enter_context(nc.Block())

        def wait_sums(eng, j, group, last_step):
            if j < 3:
                eng.wait_ge(acc_done, group * 3 + (j + 1))
            else:
                eng.wait_ge(step_done, last_step + 1)

        G_MERGE = 2 * NH
        G_OUT = G_MERGE + 4 * NC_
        G_PLE = G_OUT + NC_
        G_GATE = G_PLE + NC_
        R_MERGE = 2 * NH
        R_OUT = R_MERGE + 2 * NC_
        R_PLE = R_OUT + NC_
        R_GATE = R_PLE + NC_

        def score_at(t):
            return P * (t * (t + 1) // 2)

        def decayed_at(t):
            return P * (t * TT - t * (t - 1) // 2)

        @block.sync
        def _(sp):
            sp.dma_start(ident[:, :], c_ident).then_inc(ident_landed, 16)
            with nc.allow_non_contiguous_dma(reason="two [2048] vectors, once"):
                sp.dma_start(gmix_col[:, :], g_mix.rearrange("l (c p) -> p (l c)", p=P)).then_inc(small_landed, 16)
                sp.dma_start(gple_col[:, :], g_ple.rearrange("l (c p) -> p (l c)", p=P)).then_inc(small_landed, 16)
            for t in range(TT):
                sp.dma_start(x_nat[:, t, :], x2d[t * P:(t + 1) * P, :]).then_inc(x_landed[t], 16)
            sp.dma_start(p_nat[:, :, :], p2d.rearrange("(t p) d -> p t d", p=P)).then_inc(p_landed, 16)
            sp.dma_start(rel_sb[:, :], rel_bias).then_inc(rel_landed, 16)
            sp.dma_start(onehot[:, :], c_onehot).then_inc(rel_landed, 16)
            sp.dma_start(mask_row[:, :], c_mask).then_inc(rel_landed, 16)

            def load(step_mod, step, src, waits=True, pairs=False):
                slot = step_mod % RAW
                if waits:
                    sp.wait_ge(lo_ready, step - (RAW - 1))
                dst = raw[:, slot, :].rearrange("p (t c) -> p t c", c=src.shape[-1])
                if pairs:
                    src = src.rearrange("(c two) t n -> two c (t n)", two=2)
                    dst = raw[:, slot, :]
                sp.dma_start(dst, src).then_inc(raw_landed[slot], 16)

            def head_weights(k, family, h):
                cols = W_in[k * P:(k + 1) * P, family * 4 * D_A:(family + 1) * 4 * D_A]
                return cols.rearrange("p (t c) -> p t c", t=4)[:, :, bass.ds(h * DH, DH)]

            def weights(W, k, n):
                return W[k * P:(k + 1) * P, bass.ds(n * CH, CH)].rearrange("p (t c) -> p t c", t=1)

            for k in range(KT):
                load(k, k, head_weights(k, 0, 0), waits=k >= RAW)
            sp.wait_ge(bias_added, 2)
            sp.dma_start(bias_row[:, :], bias_vec[:, :]).then_inc(bias_stored, 16)
            sp.wait_ge(bias_stored, 16)
            sp.dma_start(bias_rep[0:NH * P * REV].rearrange("(h i r) -> h i r", h=NH, i=P),
                         bias_row[:, :].rearrange("h (i r) -> h i r", i=1).to_broadcast([NH, P, REV])
                         ).then_inc(bias_spread, 16)

            def bias_table(h):
                first = bias_rep[bass.ds(h * (P * REV) + (P - 1), P * (REV - 1))]
                return first.rearrange("(i r) -> i r", r=REV - 1)[:, 0:S]

            with sp.Fori(1, NH) as h:
                for k in range(KT):
                    load(k, h * KT + k, head_weights(k, 0, h))
                    if k == 2:
                        sp.wait_ge(x_turned, KT)
                        sp.wait_ge(bias_spread, 16)
                        sp.dma_start(table[:, :], bias_table(h - 1)).then_inc(table_landed, 16)
            for k in range(KT):
                load(k, NH * KT + k, head_weights(k, 1, 0))
                if k == 0:
                    sp.wait_ge(probs_ready, TT * (NH - 1))
                    sp.dma_start(table[:, :], bias_table(NH - 1)).then_inc(table_landed, 16)
                    sp.dma_start(cos_sb[:, :], c_cos).then_inc(rot_landed, 16)
                    sp.dma_start(sin_sb[:, :], c_sin).then_inc(rot_landed, 16)
            with sp.Fori(1, NH) as h:
                for k in range(KT):
                    load(k, h * KT + (NH * KT + k), head_weights(k, 1, h))
                    if k == 0:
                        sp.wait_ge(probs_ready, h * TT + TT * (NH - 1))
                        sp.dma_start(table[:, :], c_decay[bass.ds(h - 1, 1), :, :].rearrange("h p c -> (h p) c")
                                     ).then_inc(table_landed, 16)

            def merge_loads(n, base, last_table):
                for k in range(KT):
                    ahead = 1 if k == KT - 1 else 0
                    sp.wait_ge(lo_ready, base + (k + ahead - (RAW - 1)))
                    load(k, base + k, weights(W_in[:, GATES:GATES + D], k, n), waits=False)
                    if last_table and k == 0:
                        sp.wait_ge(probs_ready, TT * (2 * NH - 1))
                        sp.dma_start(table[:, :], c_decay[NH - 1]).then_inc(table_landed, 16)
                for k in range(KY):
                    load(k, base + (KT + k), weights(W_a, k, n), waits=k > 0)
                for k in range(KT):
                    load(k, base + (KT + KY + k), weights(W_in[:, GATES + D:GATES + 2 * D], k, n))
                for k in range(KY):
                    load(k, base + (2 * KT + KY + k), weights(W_b, k, n), pairs=True)

            merge_loads(0, HEAD_STEPS, True)
            with sp.Fori(1, NC_) as n:
                merge_loads(n, n * MERGE_STEPS + HEAD_STEPS, False)
            with sp.Fori(0, NC_) as n:
                for k in range(KT):
                    load(k, n * KT + (OUT0 + k), weights(W_out, k, n))
            for n in range(NC_):
                for k in range(2):
                    load(PLE0 + 2 * n + k, PLE0 + 2 * n + k, weights(W_pp, k, n))
            for k in range(KT):
                load(k, GATE0 + k, weights(W_pg, k, 0))
            sp.wait_ge(step_done, PLE0)
            sp.dma_start(gfin[:, :], g_final.rearrange("(o d) -> o d", o=1).to_broadcast([P, D])
                         ).then_inc(gfin_landed, 16)
            with sp.Fori(1, NC_) as n:
                for k in range(KT):
                    load(k, n * KT + (GATE0 + k), weights(W_pg, k, n))
            for t in range(TT):
                sp.wait_ge(out_ready, t + 1)
                sp.dma_start(out2d[t * P:(t + 1) * P, :], x_res[:, t, :]).then_inc(out_stored, 16)
            sp.wait_ge(out_stored, 16 * TT)

        @block.tensor
        def _(pe):
            def passes(acc, st_hi, st_lo, mv_hi, mv_lo, first, last):
                pe.matmul(acc, st_hi, mv_hi, start=first, stop=False)
                pe.matmul(acc, st_hi, mv_lo, start=False, stop=False)
                return pe.matmul(acc, st_lo, mv_hi, start=False, stop=last)

            def parts_ready(step):
                pe.wait_ge(hi_ready, step + 1)
                pe.wait_ge(lo_ready, step + 1)

            def transposed_step(step_mod, step, accs, a_hi, a_lo, first, last, free=None):
                slot = step_mod % SPLIT
                parts_ready(step)
                for j in range(4):
                    if first and free is not None:
                        free(j)
                    hi, lo = w_hi[:, slot, j * P:(j + 1) * P], w_lo[:, slot, j * P:(j + 1) * P]
                    mm = passes(accs[j][:, :], hi, lo, a_hi, a_lo, first, last)
                    if last and j < 3:
                        mm.then_inc(acc_done, 1)
                mm.then_inc(step_done, 1)

            def natural_step(step_mod, step, accs, a_hi, a_lo, first, last, free=None):
                slot = step_mod % SPLIT
                parts_ready(step)
                for t in range(TT):
                    if first and free is not None:
                        free(t)
                    mm = passes(accs[t][:, :], a_hi[:, t * P:(t + 1) * P], a_lo[:, t * P:(t + 1) * P],
                                w_hi[:, slot, :], w_lo[:, slot, :], first, last)
                    if last and t < 3:
                        mm.then_inc(acc_done, 1)
                mm.then_inc(step_done, 1)

            low, high = bank[0:4], bank[4:8]

            pe.wait_ge(rel_landed, 48)
            for i in range(2):
                half = slice(i * REV // 2, (i + 1) * REV // 2)
                pe.matmul(bank[i][0:NH, 0:REV // 2], rel_sb[:, :], onehot[:, half],
                          start=True, stop=True).then_inc(bias_mm, 1)
            pe.wait_ge(ident_landed, 16)
            pe.wait_ge(p_landed, 16)
            for c in range(2):
                for t in range(TT):
                    mm = pe.transpose(bank[2 + c][:, t * P:(t + 1) * P], p_nat[:, t, c * P:(c + 1) * P], ident[:, :])
                mm.then_inc(p_turned, 1)

            def turn_x(c):
                if c >= 4:
                    pe.wait_ge(h_lo, c - 3)
                for t in range(TT):
                    if c == 0:
                        pe.wait_ge(scaled, t + 1)
                    mm = pe.transpose(high[c % 4][:, t * P:(t + 1) * P], x_nat[:, t, c * P:(c + 1) * P], ident[:, :])
                mm.then_inc(x_turned, 1)

            def values_turned(J):
                pe.wait_ge(bank_read[2], J + 1)
                for t in range(TT):
                    mm = pe.transpose(high[3][:, t * P:(t + 1) * P], v_sb[:, t * P:(t + 1) * P], ident[:, :])
                mm.then_inc(v_turned, 1)

            def attention(k, J):
                if k == 0:
                    pe.wait_ge(y_ready, J + 1)
                    values_turned(J)
                if k == 1:
                    pe.wait_ge(bank_read[0], J + 1)
                    pe.wait_ge(bank_read[1], J + 1)
                    pe.wait_ge(k_mean_ready, J + 1)
                    for i in range(2):
                        pe.matmul(high[0][:, CH - 2 + i:CH - 1 + i], q_sb[:, (2 + i) * P:(3 + i) * P], k_mean[:, :],
                                  start=True, stop=True)
                    for t in range(3):
                        pe.matmul(high[t][:, 0:(t + 1) * P], q_sb[:, t * P:(t + 1) * P], k_sb[:, 0:(t + 1) * P],
                                  start=True, stop=True).then_inc(scores_done, 1)
                if k == 2:
                    pe.wait_ge(v_nat_ready, J + 1)
                    pe.matmul(high[3][:, :], q_sb[:, 3 * P:4 * P], k_sb[:, :],
                              start=True, stop=True).then_inc(scores_done, 1)
                for t, at_k in enumerate((7, 8, 9, 10)):
                    if k == at_k:
                        pe.wait_ge(probs_ready, J * TT + (t + 1))
                        for kt in range(t + 1):
                            a = score_at(t) + kt * P
                            mm = pe.transpose(high[t][:, kt * P:(kt + 1) * P], probs[:, a:a + P], ident[:, :])
                        mm.then_inc(p_turn, 1)
                if k == 12:
                    pe.wait_ge(pT_act, J * 2 + 2)
                    pe.wait_ge(pT_dve, J * 2 + 2)
                    for kt in range(TT):
                        mm = pe.matmul(high[0][:, kt * P:], v_nat[:, kt, :], probsT[:, kt, kt * P:],
                                       start=(kt == 0), stop=(kt == TT - 1))
                    mm.then_inc(pv_done, 1)

            def retention(k, J):
                if k == 0:
                    pe.wait_ge(y_ready, J + 1)
                    values_turned(J)
                if k == 3:
                    pe.wait_ge(rotated, (J - NH) * 2 + 3)
                    pe.wait_ge(v_nat_ready, J + 1)
                    for kt in range(TT):
                        pe.matmul(high[kt][:, 0:S - kt * P], k_sb[:, kt * P:(kt + 1) * P], q_sb[:, kt * P:],
                                  start=True, stop=True).then_inc(scores_done, 1)
                if k == 8:
                    pe.wait_ge(probs_ready, J * TT + TT)
                    for kt in range(TT):
                        a = decayed_at(kt)
                        mm = pe.matmul(high[0][:, kt * P:], v_nat[:, kt, :], probs[:, a:a + S - kt * P],
                                       start=(kt == 0), stop=(kt == TT - 1))
                    mm.then_inc(pv_done, 1)
                if k == 10:
                    pe.wait_ge(osq_ready, J - NH + 1)
                    pe.matmul(high[1][:, :], ones[:, :], o_sq[:, :], start=True, stop=True).then_inc(mean_done, 1)

            def head_group(G, job):
                def free(j):
                    if not (isinstance(G, int) and G == 0):
                        pe.wait_ge(bank_read[j], G)
                    elif j < 2:
                        pe.wait_ge(bias_added, j + 1)
                    else:
                        pe.wait_ge(p_lo, j - 1)
                for k in range(KT):
                    if isinstance(G, int) and G == 0:
                        pe.wait_ge(h_hi, k + 1)
                        pe.wait_ge(h_lo, k + 1)
                    transposed_step(k, G * KT + k, low, hT_hi[:, k, :], hT_lo[:, k, :], k == 0, k == KT - 1,
                                         free)
                    job(k)

            for c in range(4):
                turn_x(c)
            head_group(0, lambda k: turn_x(k + 4) if k + 4 < KT else None)
            with pe.Fori(1, NH) as h:
                head_group(h, lambda k: attention(k, h - 1))
            head_group(NH, lambda k: attention(k, NH - 1))
            with pe.Fori(NH + 1, 2 * NH) as G:
                head_group(G, lambda k: retention(k, G - 1))

            def merge_group(n, base, job):
                def free_low(g):
                    return lambda j: pe.wait_ge(bank_read[j], g)

                def free_high(g, always):
                    return lambda j: pe.wait_ge(merge_read[j], g) if always else None
                for k in range(KT):
                    transposed_step(k, base + k, low, hT_hi[:, k, :], hT_lo[:, k, :], k == 0, k == KT - 1,
                                         free_low(2 * n + R_MERGE))
                    job(k)
                first_chunk = isinstance(n, int) and n == 0
                for k in range(KY):
                    if first_chunk and k == 0:
                        pe.wait_ge(y_hi, NH)
                        pe.wait_ge(y_lo, NH)
                        pe.wait_ge(y_ready, 2 * NH + 1)
                    transposed_step(k, base + (KT + k), high, yT_hi[:, k, :], yT_lo[:, k, :], k == 0, k == KY - 1,
                                         free_high(2 * n, not first_chunk))
                for k in range(KT):
                    transposed_step(k, base + (KT + KY + k), low, hT_hi[:, k, :], hT_lo[:, k, :], k == 0,
                                         k == KT - 1, free_low(2 * n + (R_MERGE + 1)))
                for k in range(KY):
                    if first_chunk and k == 0:
                        pe.wait_ge(y_hi, 2 * NH)
                        pe.wait_ge(y_lo, 2 * NH)
                    transposed_step(k, base + (2 * KT + KY + k), high, yT_hi[:, KY + k, :], yT_lo[:, KY + k, :],
                                         k == 0, k == KY - 1, free_high(2 * n + 1, True))

            merge_group(0, HEAD_STEPS, lambda k: retention(k, 2 * NH - 1))
            with pe.Fori(1, NC_) as n:
                merge_group(n, n * MERGE_STEPS + HEAD_STEPS, lambda k: None)

            def turn_x1(n, i):
                for t in range(TT):
                    pe.wait_ge(bank_read[t], R_OUT + n + 1)
                if n == 0:
                    pe.wait_ge(merge_read[i], 2 * NC_)
                else:
                    pe.wait_ge(hp_lo, n * 4 + (i - 3))
                for t in range(TT):
                    mm = pe.transpose(high[i][:, t * P:(t + 1) * P],
                                      x_res[:, t, n * CH + i * P:n * CH + (i + 1) * P], ident[:, :])
                mm.then_inc(x1_turned, 1)

            def out_chunk(n, job):
                def free(t):
                    pe.wait_ge(bank_read[t], R_OUT + n)
                for k in range(KT):
                    if isinstance(n, int) and n == 0:
                        pe.wait_ge(m_hi, k + 1)
                        pe.wait_ge(m_lo, k + 1)
                    natural_step(k, n * KT + (OUT0 + k), low, hT_hi[:, k, :], hT_lo[:, k, :],
                                      k == 0, k == KT - 1, free)
                    job(k)

            out_chunk(0, lambda k: None)
            for n in range(1, NC_):
                out_chunk(n, lambda k: turn_x1(n - 1, (k - 3) // 3) if k in (3, 6, 9, 12) else None)
            for n in range(NC_):
                def free(t):
                    pe.wait_ge(bank_read[t], R_PLE + n)
                for k in range(2):
                    step = PLE0 + 2 * n + k
                    natural_step(step, step, low, pT_hi[:, k, :], pT_lo[:, k, :], k == 0, k == 1, free)
                    if k == 1:
                        turn_x1(NC_ - 1, n)

            def gate_chunk(n):
                def free(t):
                    pe.wait_ge(bank_read[t], n + R_GATE)
                for k in range(KT):
                    if isinstance(n, int) and n == 0:
                        pe.wait_ge(hp_hi, k + 1)
                        pe.wait_ge(hp_lo, k + 1)
                    natural_step(k, n * KT + (GATE0 + k), low, yT_hi[:, k, :], yT_lo[:, k, :],
                                      k == 0, k == KT - 1, free)

            gate_chunk(0)
            with pe.Fori(1, NC_) as n:
                gate_chunk(n)

        def tile_landed(eng, mod, step):
            use = step // RAW * 16 if isinstance(step, int) else (step - mod) * (16 // RAW)
            eng.wait_ge(raw_landed[mod], use + 16)

        def parts_free(eng, step):
            if not (isinstance(step, int) and step < SPLIT):
                eng.wait_ge(step_done, step - (SPLIT - 1))

        def raw_view(tile, pairs):
            return tile.rearrange("p (j c two) -> p j two c", j=4, two=2) if pairs else tile

        def split_view(tile, pairs):
            return tile.rearrange("p (j two c) -> p j two c", j=4, two=2) if pairs else tile

        @block.scalar
        def _(act):
            def split_hi(mod, step, pairs=False):
                if isinstance(step, int) and step >= STEPS:
                    return
                mod = mod % RAW
                tile_landed(act, mod, step)
                parts_free(act, step)
                act.activation(split_view(w_hi[:, mod % SPLIT, :], pairs), raw_view(raw[:, mod, :], pairs), COPY
                               ).then_inc(hi_ready, 1)

            act.wait_ge(ones_set, 2)
            for t in range(TT):
                act.wait_ge(x_landed[t], 16)
                act.activation(sq_junk[:, :], x_nat[:, t, :], ACT.Square, accum_out=sq_x[:, t:t + 1]).then_inc(sq_done, 1)
                act.wait_ge(sq_done, t + 1)
                act.activation(rms_x[:, t:t + 1], sq_x[:, t:t + 1], ACT.Sqrt, bias=eps_col[:, :], scale=1.0 / D
                               ).then_inc(rms_done, 1)
            for c in range(2):
                act.wait_ge(p_turned, c + 1)
                act.activation(pT_hi[:, c, :], bank[2 + c][:, :], COPY).then_inc(p_hi, 1)
            for k in range(LEAD):
                split_hi(k, k)

            def h_part(c):
                act.wait_ge(x_turned, c + 1)
                act.wait_ge(small_landed, 32)
                act.activation(hT_hi[:, c, :], bank[4 + c % 4][:, :], COPY, scale=gmix_col[:, c:c + 1]).then_inc(h_hi, 1)

            def attention(k, J):
                if k == 1:
                    act.wait_ge(v_turned, J + 1)
                    act.activation(v_nat[:, :, :].rearrange("p t d -> p (t d)"), bank[7][:, :], COPY).then_inc(v_nat_ready, 1)
                for t in range(TT):
                    if k == 3 + t:
                        act.wait_ge(max_ready, J * TT + (t + 1))
                        a, n = score_at(t), (t + 1) * P
                        act.activation(probs[:, a:a + n], probs[:, a:a + n], ACT.Exp, bias=neg_max[:, t:t + 1],
                                       accum_out=row_sum[:, t:t + 1]).then_inc(exp_done, 1)
                for t, at_k in ((0, 8), (2, 10)):
                    if k == at_k:
                        act.wait_ge(p_turn, J * TT + (t + 1))
                        act.activation(probsT[:, 0:t + 1, t * P:(t + 1) * P],
                                       bank[4 + t][:, 0:(t + 1) * P].rearrange("p (k q) -> p k q", q=P), COPY
                                       ).then_inc(pT_act, 1)
                y_part(k, J)

            def y_part(k, J):
                if k == 14:
                    act.wait_ge(y_ready, J + 2)
                    act.activation(yT_hi[:, bass.ds(J, 1), :].rearrange("p j s -> p (j s)"), y32[:, :], COPY).then_inc(y_hi, 1)

            def retention(k, J):
                if k == 1:
                    act.wait_ge(v_turned, J + 1)
                    act.activation(v_nat[:, :, :].rearrange("p t d -> p (t d)"), bank[7][:, :], COPY).then_inc(v_nat_ready, 1)
                if k == 9:
                    act.wait_ge(pv_done, J + 1)
                    act.activation(o_sq[:, :], bank[4][:, :], ACT.Square).then_inc(osq_ready, 1)
                if k == 11:
                    act.wait_ge(mean_done, J - (NH - 1))
                    act.activation(o_rms[:, :], bank[5][:, :], ACT.Sqrt, bias=eps_col[:, :]).then_inc(root_ready, 1)
                y_part(k, J)

            def head_group(G, job, pairs, next_pairs):
                first = isinstance(G, int) and G == 0
                for k in range(KT):
                    split_hi(k + LEAD, G * KT + (k + LEAD), pairs if k + LEAD < KT else next_pairs)
                    job(k)
                wait_sums(act, 0, G, None)
                if not first:
                    act.wait_ge(scores_done, G * TT)
                act.activation(q_sb[:, :], bank[0][:, :], COPY, scale=float(DH) ** -0.5).then_inc(bank_read[0], 1)
                wait_sums(act, 2, G, None)
                if not first:
                    act.wait_ge(v_turned, G)
                act.activation(v_sb[:, :], bank[2][:, :], COPY).then_inc(bank_read[2], 1)
                act.wait_ge(bank_read[3], G + 1)
                if not first:
                    act.wait_ge(zs_ready, G)
                act.activation(z_tanh[:, :], z_half[:, :], ACT.Tanh).then_inc(tanh_ready, 1)

            for c in range(4):
                h_part(c)
            head_group(0, lambda k: h_part(k + 4) if k + 4 < KT else None, False, False)
            with act.Fori(1, NH - 1) as h:
                head_group(h, lambda k: attention(k, h - 1), False, False)
            head_group(NH - 1, lambda k: attention(k, NH - 2), False, True)
            head_group(NH, lambda k: attention(k, NH - 1), True, True)
            with act.Fori(NH + 1, 2 * NH - 1) as G:
                head_group(G, lambda k: retention(k, G - 1), True, True)
            head_group(2 * NH - 1, lambda k: retention(k, 2 * NH - 2), True, False)

            def merge_group(n, base, job):
                first_chunk = isinstance(n, int) and n == 0
                for k in range(KT):
                    split_hi(k + LEAD, base + (k + LEAD))
                    job(k)
                for j in range(4):
                    wait_sums(act, j, n * 4 + G_MERGE, base + (KT - 1))
                    if not first_chunk:
                        act.wait_ge(merged_ready, n * 4 + (j - 3))
                    act.activation(g_tanh[:, j, :], bank[j][:, :], ACT.Tanh, scale=0.5).then_inc(bank_read[j], 1)
                for k in range(KY + KT):
                    split_hi(k + LEAD, base + (KT + k + LEAD))
                for j in range(4):
                    wait_sums(act, j, n * 4 + (G_MERGE + 2), base + (2 * KT + KY - 1))
                    act.wait_ge(merge_read[j], n * 2 + 1)
                    act.activation(g_tanh[:, j, :], bank[j][:, :], ACT.Tanh, scale=0.5).then_inc(bank_read[j], 1)
                for k in range(KY):
                    split_hi(k + LEAD, base + (2 * KT + KY + k + LEAD))

            merge_group(0, HEAD_STEPS, lambda k: retention(k, 2 * NH - 1))
            with act.Fori(1, NC_) as n:
                merge_group(n, n * MERGE_STEPS + HEAD_STEPS, lambda k: None)

            def merged_part(c):
                act.wait_ge(merged_ready, c + 1)
                if c == 0:
                    act.wait_ge(step_done, OUT0 - KY)
                act.activation(hT_hi[:, c, :], merged[:, c, :], COPY, scale=0.5).then_inc(m_hi, 1)

            def hp_part(c):
                act.wait_ge(x1_turned, c + 1)
                act.activation(yT_hi[:, c, :], bank[4 + c % 4][:, :], COPY, scale=gple_col[:, c:c + 1]).then_inc(hp_hi, 1)

            def x1_square(n, t):
                act.wait_ge(bank_read[t], R_OUT + n + 1)
                if n or t:
                    act.wait_ge(x1_sq, n * TT + t)
                act.activation(junk[:, :], x_res[:, t, n * CH:(n + 1) * CH], ACT.Square,
                               accum_out=sq1[:, t, n:n + 1]).then_inc(x1_sq, 1)

            for c in range(4):
                merged_part(c)
            for n in range(NC_):
                for k in range(KT):
                    split_hi(k + LEAD, OUT0 + n * KT + k + LEAD)
                    if n == 0:
                        for c in (4 + 2 * k, 5 + 2 * k):
                            if c < KT:
                                merged_part(c)
                        if k == 7:
                            act.wait_ge(m_lo, KT)
                            for t in range(TT):
                                act.dma_start(x_res[:, t, :], x2d[t * P:(t + 1) * P, :]).then_inc(xres_landed, 16)
                    else:
                        if k in (0, 1, 2, 3):
                            x1_square(n - 1, k)
                        if k in (4, 7, 10, 13):
                            hp_part((n - 1) * 4 + (k - 4) // 3)
            for n in range(NC_):
                for k in range(2):
                    step = PLE0 + 2 * n + k
                    split_hi(step + LEAD, step + LEAD)
                for t in range(TT):
                    if n == 0:
                        x1_square(NC_ - 1, t)
                for t in range(TT):
                    wait_sums(act, t, G_PLE + n, PLE0 + 2 * n + 1)
                    act.activation(ple[:, t, n * CH:(n + 1) * CH], bank[t][:, :], COPY, scale=0.5).then_inc(bank_read[t], 1)
                hp_part(12 + n)
            act.wait_ge(sum1_ready, 1)
            act.activation(rms1[:, :], sum1[:, :], ACT.Sqrt, bias=eps_col[:, :], scale=1.0 / D).then_inc(rms1_ready, 1)

            def gate_chunk(n):
                for k in range(KT):
                    if not (isinstance(n, int) and n == NC_ - 1 and k >= KT - LEAD):
                        split_hi(k + LEAD, n * KT + (GATE0 + k + LEAD))
                for t in range(TT):
                    if isinstance(n, int) and n == 0:
                        act.wait_ge(half1_ready, 1)
                    else:
                        act.wait_ge(x2_ready, n * TT + (t - 3))
                    wait_sums(act, t, n + G_GATE, n * KT + (GATE0 + KT - 1))
                    act.activation(pg_tanh[:, t, :], bank[t][:, :], ACT.Tanh, scale=half1[:, t:t + 1]
                                   ).then_inc(bank_read[t], 1)
                for t in range(TT):
                    act.wait_ge(x2_ready, n * TT + (t + 1))
                    if t or not (isinstance(n, int) and n == 0):
                        act.wait_ge(x2_sq, n * TT + t)
                    act.activation(junk2[:, :], x_res[:, t, bass.ds(n * CH, CH)], ACT.Square,
                                   accum_out=sq2[:, t, bass.ds(n, 1)]).then_inc(x2_sq, 1)

            gate_chunk(0)
            with act.Fori(1, NC_ - 1) as n:
                gate_chunk(n)
            gate_chunk(NC_ - 1)
            act.wait_ge(sum2_ready, 1)
            act.activation(rms2[:, :], sum2[:, :], ACT.Sqrt, bias=eps_col[:, :], scale=1.0 / D).then_inc(rms2_ready, 1)

        @block.vector
        def _(dve):
            def split_lo(mod, step, pairs=False):
                if isinstance(step, int) and step >= STEPS:
                    return
                mod = mod % RAW
                tile_landed(dve, mod, step)
                parts_free(dve, step)
                dve.wait_ge(hi_ready, step + 1)
                dve.tensor_tensor(split_view(w_lo[:, mod % SPLIT, :], pairs), raw_view(raw[:, mod, :], pairs),
                                  split_view(w_hi[:, mod % SPLIT, :].bitcast(F32), pairs),
                                  ALU.subtract).then_inc(lo_ready, 1)

            dve.memset(eps_col[:, :], EPS).then_inc(ones_set, 1)
            dve.memset(ones[:, :], 1.0 / P).then_inc(ones_set, 1)
            dve.memset(k_sum[:, :], 0.0).then_inc(y_ready, 1)
            dve.memset(k_mean[:, :], 0.0).then_inc(rotated, 1)
            for t in range(TT):
                dve.wait_ge(rms_done, t + 1)
                dve.reciprocal(inv_x[:, t:t + 1], rms_x[:, t:t + 1]).then_inc(inv_done, 1)
                dve.wait_ge(inv_done, t + 1)
                dve.tensor_scalar(x_nat[:, t, :], x_nat[:, t, :], inv_x[:, t:t + 1], None, ALU.mult).then_inc(scaled, 1)
            for i in range(2):
                half = slice(i * REV // 2, (i + 1) * REV // 2)
                dve.wait_ge(bias_mm, i + 1)
                dve.tensor_tensor(bias_vec[:, half], bank[i][0:NH, 0:REV // 2], mask_row[:, half], ALU.add
                                  ).then_inc(bias_added, 1)
            for c in range(2):
                dve.wait_ge(p_hi, c + 1)
                dve.tensor_tensor(pT_lo[:, c, :], bank[2 + c][:, :], pT_hi[:, c, :].bitcast(F32), ALU.subtract
                                  ).then_inc(p_lo, 1)
            for k in range(LEAD):
                split_lo(k, k)

            def h_part(c):
                dve.wait_ge(h_hi, c + 1)
                dve.scalar_tensor_tensor(out=hT_lo[:, c, :], in0=bank[4 + c % 4][:, :], scalar=gmix_col[:, c:c + 1],
                                         in1=hT_hi[:, c, :].bitcast(F32), op0=ALU.mult, op1=ALU.subtract
                                         ).then_inc(h_lo, 1)

            def silu(J):
                dve.wait_ge(tanh_ready, J + 1)
                dve.scalar_tensor_tensor(out=z_half[:, :], in0=z_tanh[:, :], scalar=1.0, in1=z_half[:, :],
                                         op0=ALU.add, op1=ALU.mult).then_inc(zs_ready, 1)

            def y_part(k, J):
                if k == 14:
                    dve.wait_ge(y_hi, J + 1)
                    dve.tensor_tensor(yT_lo[:, bass.ds(J, 1), :].rearrange("p j s -> p (j s)"), y32[:, :],
                                      yT_hi[:, bass.ds(J, 1), :].rearrange("p j s -> p (j s)").bitcast(F32),
                                      ALU.subtract).then_inc(y_lo, 1)

            def attention(k, J):
                if k == 0:
                    dve.wait_ge(bank_read[1], J + 1)
                    dve.tensor_reduce(k_sum[:, :], k_sb[:, 0:BLOCK], AX.X, ALU.add).then_inc(k_summed, 1)
                    dve.wait_ge(k_summed, J + 1)
                    dve.tensor_scalar(k_mean[:, :], k_sum[:, :], float(DH) ** 0.5 / BLOCK, None, ALU.mult
                                      ).then_inc(k_mean_ready, 1)
                    silu(J)
                if k == 2:
                    dve.wait_ge(scores_done, J * TT + 1)
                    dve.tensor_scalar(finite[:, :], bank[4][:, CH - 2:CH], 0.0, 0.0, ALU.mult, ALU.is_equal
                                      ).then_inc(gate_finite, 1)
                    dve.wait_ge(gate_finite, J + 1)
                    dve.tensor_scalar(cap[:, :], finite[:, :], 2 * BIG, -BIG, ALU.mult, ALU.add).then_inc(cap_ready, 1)
                for t in range(TT):
                    a, n = score_at(t), (t + 1) * P
                    tab = (TT - 1 - t) * P
                    if k == 2 + t:
                        dve.wait_ge(scores_done, J * TT + (t + 1))
                        dve.wait_ge(table_landed, J * 16 + 16)
                        past = BLOCK if t * P >= BLOCK else 0
                        if past:
                            dve.wait_ge(cap_ready, J + 1)
                            dve.scalar_tensor_tensor(out=probs[:, a:a + past], in0=bank[4 + t][:, 0:past],
                                                     scalar=cap[:, t - 2:t - 1], in1=table[:, tab:tab + past],
                                                     op0=ALU.min, op1=ALU.add).then_inc(biased, 1)
                        dve.tensor_tensor(probs[:, a + past:a + n], bank[4 + t][:, past:n], table[:, tab + past:tab + n],
                                          ALU.add).then_inc(biased, 1)
                        dve.wait_ge(biased, J * 6 + (1, 2, 4, 6)[t])
                        dve.tensor_reduce(neg_max[:, t:t + 1], probs[:, a:a + n], AX.X, ALU.max, negate=True
                                          ).then_inc(max_ready, 1)
                    if k == 4 + t:
                        dve.wait_ge(exp_done, J * TT + (t + 1))
                        dve.reciprocal(row_inv[:, t:t + 1], row_sum[:, t:t + 1]).then_inc(inv_ready, 1)
                        dve.wait_ge(inv_ready, J * TT + (t + 1))
                        dve.tensor_scalar(probs[:, a:a + n], probs[:, a:a + n], row_inv[:, t:t + 1], None, ALU.mult
                                          ).then_inc(probs_ready, 1)
                for t, at_k in ((1, 9), (3, 11)):
                    if k == at_k:
                        dve.wait_ge(p_turn, J * TT + (t + 1))
                        dve.tensor_copy(probsT[:, 0:t + 1, t * P:(t + 1) * P],
                                        bank[4 + t][:, 0:(t + 1) * P].rearrange("p (k q) -> p k q", q=P)
                                        ).then_inc(pT_dve, 1)
                if k == 13:
                    dve.wait_ge(pv_done, J + 1)
                    dve.tensor_tensor(y32[:, :], bank[4][:, :], z_half[:, :], ALU.mult).then_inc(y_ready, 1)
                y_part(k, J)

            def retention(k, J):
                b = J - NH
                if k == 0:
                    silu(J)
                    dve.wait_ge(rot_landed, 32)
                for i, src in enumerate((q_sb, k_sb)):
                    if k == i:
                        dve.wait_ge(bank_read[i], J + 1)
                        dve.wait_ge(rotated, b * 2 + (i + 1))
                        dve.tensor_tensor(rot_cos[:, :], src[:, :], cos_sb[:, :], ALU.mult).then_inc(rot_cos_done, 1)
                        for lo, hi in ((0, 64), (64, 0)):
                            dve.tensor_tensor(rot_sin[lo:lo + 64, :], src[hi:hi + 64, :], sin_sb[hi:hi + 64, :], ALU.mult
                                              ).then_inc(rot_sin_done, 1)
                        dve.wait_ge(rot_cos_done, b * 2 + (i + 1))
                        dve.wait_ge(rot_sin_done, b * 4 + (2 * i + 2))
                        dve.tensor_tensor(src[:, :], rot_cos[:, :], rot_sin[:, :], ALU.add).then_inc(rotated, 1)
                for kt in range(TT):
                    if k == 4 + kt // 2:
                        a, n = decayed_at(kt), S - kt * P
                        dve.wait_ge(scores_done, J * TT + (kt + 1))
                        dve.wait_ge(table_landed, J * 16 + 16)
                        dve.tensor_tensor(probs[:, a:a + n], bank[4 + kt][:, 0:n], table[:, 0:n], ALU.mult
                                          ).then_inc(probs_ready, 1)
                if k == 12:
                    dve.wait_ge(root_ready, b + 1)
                    dve.reciprocal(o_inv[:, :], o_rms[:, :]).then_inc(oinv_ready, 1)
                    dve.tensor_tensor(y32[:, :], bank[4][:, :], z_half[:, :], ALU.mult).then_inc(gated, 1)
                    dve.wait_ge(oinv_ready, b + 1)
                    dve.wait_ge(gated, b + 1)
                    dve.tensor_tensor(y32[:, :], y32[:, :], o_inv[:, :], ALU.mult).then_inc(y_ready, 1)
                y_part(k, J)

            def head_group(G, job, pairs, next_pairs):
                first = isinstance(G, int) and G == 0
                for k in range(KT):
                    split_lo(k + LEAD, G * KT + (k + LEAD), pairs if k + LEAD < KT else next_pairs)
                    job(k)
                wait_sums(dve, 1, G, None)
                if not first:
                    dve.wait_ge(scores_done, G * TT)
                dve.tensor_copy(k_sb[:, :], bank[1][:, :]).then_inc(bank_read[1], 1)
                wait_sums(dve, 3, G, G * KT + (KT - 1))
                dve.tensor_scalar(z_half[:, :], bank[3][:, :], 0.5, None, ALU.mult).then_inc(bank_read[3], 1)

            for c in range(4):
                h_part(c)
            head_group(0, lambda k: h_part(k + 4) if k + 4 < KT else None, False, False)
            with dve.Fori(1, NH - 1) as h:
                head_group(h, lambda k: attention(k, h - 1), False, False)
            head_group(NH - 1, lambda k: attention(k, NH - 2), False, True)
            head_group(NH, lambda k: attention(k, NH - 1), True, True)
            with dve.Fori(NH + 1, 2 * NH - 1) as G:
                head_group(G, lambda k: retention(k, G - 1), True, True)
            head_group(2 * NH - 1, lambda k: retention(k, 2 * NH - 2), True, False)

            def merge_group(n, base, job):
                for k in range(KT):
                    split_lo(k + LEAD, base + (k + LEAD))
                    job(k)
                for k in range(KY):
                    split_lo(k + LEAD, base + (KT + k + LEAD))
                for j in range(4):
                    wait_sums(dve, j, n * 4 + (G_MERGE + 1), base + (KT + KY - 1))
                    dve.wait_ge(bank_read[j], n * 2 + (R_MERGE + 1))
                    dve.scalar_tensor_tensor(out=merged[:, bass.ds(n * 4 + j, 1), :].rearrange("p j s -> p (j s)"),
                                             in0=g_tanh[:, j, :], scalar=1.0, in1=bank[4 + j][:, :],
                                             op0=ALU.add, op1=ALU.mult).then_inc(merge_read[j], 1)
                for k in range(KT + KY):
                    split_lo(k + LEAD, base + (KT + KY + k + LEAD))
                for j in range(4):
                    wait_sums(dve, j, n * 4 + (G_MERGE + 3), base + (MERGE_STEPS - 1))
                    dve.wait_ge(bank_read[j], n * 2 + (R_MERGE + 2))
                    dve.scalar_tensor_tensor(out=g_tanh[:, j, :], in0=g_tanh[:, j, :], scalar=1.0,
                                             in1=bank[4 + j][:, :], op0=ALU.add, op1=ALU.mult).then_inc(merge_read[j], 1)
                    dve.wait_ge(merge_read[j], n * 2 + 2)
                    tile = merged[:, bass.ds(n * 4 + j, 1), :].rearrange("p j s -> p (j s)")
                    dve.tensor_tensor(tile, tile, g_tanh[:, j, :], ALU.add).then_inc(merged_ready, 1)

            merge_group(0, HEAD_STEPS, lambda k: retention(k, 2 * NH - 1))
            with dve.Fori(1, NC_) as n:
                merge_group(n, n * MERGE_STEPS + HEAD_STEPS, lambda k: None)

            def merged_part(c):
                dve.wait_ge(m_hi, c + 1)
                dve.scalar_tensor_tensor(out=hT_lo[:, c, :], in0=merged[:, c, :], scalar=0.5,
                                         in1=hT_hi[:, c, :].bitcast(F32), op0=ALU.mult, op1=ALU.subtract
                                         ).then_inc(m_lo, 1)

            def hp_part(c):
                dve.wait_ge(hp_hi, c + 1)
                dve.scalar_tensor_tensor(out=yT_lo[:, c, :], in0=bank[4 + c % 4][:, :], scalar=gple_col[:, c:c + 1],
                                         in1=yT_hi[:, c, :].bitcast(F32), op0=ALU.mult, op1=ALU.subtract
                                         ).then_inc(hp_lo, 1)

            for c in range(4):
                merged_part(c)
            for n in range(NC_):
                for k in range(KT):
                    split_lo(k + LEAD, OUT0 + n * KT + k + LEAD)
                    if n == 0:
                        for c in (4 + 2 * k, 5 + 2 * k):
                            if c < KT:
                                merged_part(c)
                    elif k in (4, 7, 10, 13):
                        hp_part((n - 1) * 4 + (k - 4) // 3)
                if n == 0:
                    dve.wait_ge(xres_landed, 16 * TT)
                for t in range(TT):
                    wait_sums(dve, t, G_OUT + n, OUT0 + n * KT + KT - 1)
                    chunk = x_res[:, t, n * CH:(n + 1) * CH]
                    dve.tensor_tensor(chunk, bank[t][:, :], chunk, ALU.add).then_inc(bank_read[t], 1)
            for n in range(NC_):
                for k in range(2):
                    step = PLE0 + 2 * n + k
                    split_lo(step + LEAD, step + LEAD)
                hp_part(12 + n)
            dve.wait_ge(x1_sq, NC_ * TT)
            dve.tensor_reduce(sum1[:, :], sq1[:, :, :], AX.X, ALU.add).then_inc(sum1_ready, 1)
            dve.wait_ge(rms1_ready, 1)
            dve.reciprocal(inv1[:, :], rms1[:, :]).then_inc(inv1_ready, 1)
            dve.wait_ge(inv1_ready, 1)
            dve.tensor_scalar(half1[:, :], inv1[:, :], 0.5, None, ALU.mult).then_inc(half1_ready, 1)

            def gate_chunk(n):
                for k in range(KT):
                    if not (isinstance(n, int) and n == NC_ - 1 and k >= KT - LEAD):
                        split_lo(k + LEAD, n * KT + (GATE0 + k + LEAD))
                for t in range(TT):
                    dve.wait_ge(bank_read[t], n + (R_GATE + 1))
                    dve.scalar_tensor_tensor(out=pg_tanh[:, t, :], in0=pg_tanh[:, t, :], scalar=1.0,
                                             in1=ple[:, t, bass.ds(n * CH, CH)], op0=ALU.add, op1=ALU.mult
                                             ).then_inc(pg_added, 1)
                    dve.wait_ge(pg_added, n * TT + (t + 1))
                    chunk = x_res[:, t, bass.ds(n * CH, CH)]
                    dve.tensor_tensor(chunk, chunk, pg_tanh[:, t, :], ALU.add).then_inc(x2_ready, 1)

            gate_chunk(0)
            with dve.Fori(1, NC_ - 1) as n:
                gate_chunk(n)
            gate_chunk(NC_ - 1)
            dve.wait_ge(x2_sq, NC_ * TT)
            dve.tensor_reduce(sum2[:, :], sq2[:, :, :], AX.X, ALU.add).then_inc(sum2_ready, 1)
            dve.wait_ge(rms2_ready, 1)
            dve.reciprocal(inv2[:, :], rms2[:, :]).then_inc(inv2_ready, 1)
            dve.wait_ge(inv2_ready, 1)
            dve.wait_ge(gfin_landed, 16)
            for t in range(TT):
                dve.scalar_tensor_tensor(out=x_res[:, t, :], in0=x_res[:, t, :], scalar=inv2[:, t:t + 1],
                                         in1=gfin[:, :], op0=ALU.mult, op1=ALU.mult).then_inc(out_ready, 1)


INPUTS = ["x", "p", "g_mix", "w_in", "w_a", "w_b", "w_out", "g_ple", "w_ple_gate", "w_ple_proj", "rel_bias",
          "g_final"]


def kernel(**inputs):
    import concourse.bacc as bacc
    from concourse.bass_utils import run_bass_kernel_spmd

    nc = bacc.Bacc("TRN2", target_bir_lowering=False, num_devices=1, dynamic_dma_scratch_size=2048)
    given = {name: np.ascontiguousarray(inputs[name]) for name in INPUTS}
    given.update(shape_constants())
    arrays, args = {}, {}
    for name, a in given.items():
        arrays[f"in_{name}"] = a
        args[name] = nc.dram_tensor(f"in_{name}", a.shape, mybir.dt.from_np(a.dtype), kind="ExternalInput").ap()
    out = nc.dram_tensor("out", inputs["x"].shape, F32, kind="ExternalOutput").ap()
    hybrid_block(nc, out=out, **args)
    result = run_bass_kernel_spmd(nc, [arrays], core_ids=[0])
    return result.results[0]["out"]
```

```python
from contextlib import ExitStack

import numpy as np
import concourse.bass as bass
from concourse import mybir

P = 128
S, D = 512, 2048
NH, DH = 8, 128
D_A = NH * DH
D_PLE = 256
EPS = 1e-6
BUCKETS, MAX_DISTANCE = 32, 128
BLOCK = 256
ROT_BASE = 10000.0

CH = 512
KT = D // P
KY = D_A // P
TT = S // P
NC_ = D // CH
RAW = 8
SPLIT = 4
LEAD = SPLIT - 1
GATES = 4 * D_A * 2
REV = 640
MASK = -1.0e30
BIG = 1.0e38

KP = D_PLE // P
HEAD0 = NC_ * KP
MERGE0 = HEAD0 + 2 * NH * KT
MERGE_STEPS = 2 * (KT + KY)
OUT0 = MERGE0 + NC_ * MERGE_STEPS
GATE0 = OUT0 + NC_ * KT
LAST0 = GATE0 + (NC_ - 1) * KT
STEPS = LAST0 + 2 * KT

F32, F32R = mybir.dt.float32, mybir.dt.float32r
ACT = mybir.ActivationFunctionType
ALU = mybir.AluOpType
AX = mybir.AxisListType
COPY = ACT.Copy


def shape_constants():
    f = np.float32
    dist = 511 - np.arange(REV)
    n = np.maximum(dist, 0)
    exact = BUCKETS // 2
    large = exact + (np.log(np.maximum(n, 1).astype(f) / f(exact)) / f(np.log(MAX_DISTANCE / exact))
                     * f(BUCKETS - exact)).astype(np.int32)
    bucket = np.where(n < exact, n, np.minimum(large, BUCKETS - 1))
    onehot = ((np.arange(BUCKETS)[:, None] == bucket[None]) & (dist >= 0)[None]).astype(f)
    mask = np.broadcast_to(np.where(dist >= 0, f(0), f(MASK)), (NH, REV)).astype(f)
    theta = (f(1) / (f(ROT_BASE) ** np.linspace(0, 1, DH // 2, dtype=f))).astype(f)
    ang = (np.arange(S, dtype=f)[:, None] * theta[None]).astype(f).T
    cos, sin = np.cos(ang).astype(f), np.sin(ang).astype(f)
    gamma = 1.0 - 2.0 ** (-5.0 - np.arange(NH))
    diff = np.arange(S)[None, :] - np.arange(P)[:, None]
    decay = np.where(diff >= 0, gamma[:, None, None] ** np.maximum(diff, 0), 0.0).astype(f)
    return {
        "c_onehot": onehot, "c_mask": mask,
        "c_cos": np.concatenate([cos, cos]), "c_sin": np.concatenate([sin, -sin]),
        "c_decay": decay, "c_ident": np.eye(P, dtype=f),
    }


def hybrid_block(nc, x, p, g_mix, w_in, w_a, w_b, w_out, g_ple, w_ple_gate, w_ple_proj, rel_bias,
                 g_final, c_onehot, c_mask, c_cos, c_sin, c_decay, c_ident, out):
    x2d = x.rearrange("b s d -> (b s) d")
    p2d = p.rearrange("l b s d -> (l b s) d")
    out2d = out.rearrange("b s d -> (b s) d")
    W_in = w_in.rearrange("l k n -> (l k) n")
    W_a = w_a.rearrange("l k n -> (l k) n")
    W_b = w_b.rearrange("l k n -> (l k) n")
    W_out = w_out.rearrange("l k n -> (l k) n")
    W_pg = w_ple_gate.rearrange("l k n -> (l k) n")
    W_pp = w_ple_proj.rearrange("l k n -> (l k) n")

    bias_row = nc.dram_tensor("bias_row", [NH, REV], F32)
    bias_rep = nc.dram_tensor("bias_rep", [NH * P * REV + REV], F32)

    ple_kept = nc.dram_tensor("ple_kept", [S, D], F32)

    top = [(nc.sbuf_base + 31) // 32 * 32]

    def at(name, shape, dt, offset):
        return nc.alloc_sbuf_tensor_at(name, shape, dt, offset=offset)

    def place(name, shape, dt=F32):
        offset = top[0]
        top[0] += (4 * int(np.prod(shape[1:])) + 31) // 32 * 32
        assert top[0] <= nc.sbuf_usable_end, (name, top[0])
        return at(name, shape, dt, offset), offset

    hT_hi, hT_at = place("hT_hi", [P, KT, S], F32R)
    hT_lo, _ = place("hT_lo", [P, KT, S], F32R)
    yT_hi, yT_at = place("yT_hi", [P, KT, S], F32R)
    yT_lo, _ = place("yT_lo", [P, KT, S], F32R)
    raw, _ = place("raw", [P, RAW, CH])
    w_hi, _ = place("w_hi", [P, SPLIT, CH], F32R)
    w_lo, _ = place("w_lo", [P, SPLIT, CH], F32R)
    pT_hi, _ = place("pT_hi", [P, 2, S], F32R)
    pT_lo, _ = place("pT_lo", [P, 2, S], F32R)
    ident, _ = place("ident", [P, P])
    ones, _ = place("ones", [P, P])
    gmix_col, _ = place("gmix_col", [P, KT])
    gple_col, _ = place("gple_col", [P, KT])
    eps_col, _ = place("eps_col", [P, 1])
    sq_x, _ = place("sq_x", [P, TT])
    rms_x, _ = place("rms_x", [P, TT])
    inv_x, _ = place("inv_x", [P, TT])
    sq1, _ = place("sq1", [P, TT, NC_])
    sum1, _ = place("sum1", [P, TT])
    rms1, _ = place("rms1", [P, TT])
    inv1, _ = place("inv1", [P, TT])
    half1, _ = place("half1", [P, TT])
    sq2, _ = place("sq2", [P, TT, NC_])
    sum2, _ = place("sum2", [P, TT])
    rms2, _ = place("rms2", [P, TT])
    inv2, _ = place("inv2", [P, TT])
    warm, _ = place("warm", [P, 2])
    k_sum, _ = place("k_sum", [P, 1])
    k_mean, _ = place("k_mean", [P, 1])
    finite, _ = place("finite", [P, 2])
    cap, _ = place("cap", [P, 2])
    neg_max, _ = place("neg_max", [P, TT])
    row_sum, _ = place("row_sum", [P, TT])
    row_inv, _ = place("row_inv", [P, TT])
    region = top[0]
    KIB = 1024
    assert region + 40 * KIB <= nc.sbuf_usable_end
    x_nat = at("x_nat", [P, TT, D], F32, region)
    p_nat = at("p_nat", [P, TT, D_PLE], F32, yT_at)
    onehot = at("onehot", [BUCKETS, REV], F32, yT_at + 4 * KIB)
    mask_row = at("mask_row", [NH, REV], F32, yT_at + 7 * KIB)
    bias_vec = at("bias_vec", [NH, REV], F32, yT_at + 10 * KIB)
    rel_sb = at("rel_sb", [BUCKETS, NH], F32, yT_at + 13 * KIB)
    q_sb = at("q_sb", [P, S], F32, region)
    k_sb = at("k_sb", [P, S], F32, region + 2 * KIB)
    v_sb = at("v_sb", [P, S], F32, region + 4 * KIB)
    z_half = at("z_half", [P, S], F32, region + 6 * KIB)
    z_tanh = at("z_tanh", [P, S], F32, region + 8 * KIB)
    v_nat = at("v_nat", [P, TT, DH], F32, region + 10 * KIB)
    probs = at("probs", [P, 10 * P], F32, region + 12 * KIB)
    probsT = at("probsT", [P, TT, S], F32, region + 17 * KIB)
    rot_cos = at("rot_cos", [P, S], F32, region + 17 * KIB)
    rot_sin = at("rot_sin", [P, S], F32, region + 19 * KIB)
    o_sq = at("o_sq", [P, S], F32, region + 21 * KIB)
    o_rms = at("o_rms", [P, S], F32, region + 23 * KIB)
    table = at("table", [P, S], F32, region + 25 * KIB)
    y32 = at("y32", [P, S], F32, region + 27 * KIB)
    cos_sb = at("cos_sb", [P, S], F32, region + 29 * KIB)
    sin_sb = at("sin_sb", [P, S], F32, region + 31 * KIB)
    sq_junk = at("sq_junk", [P, D], F32, yT_at + 16 * KIB)
    ple_out = at("ple_out", [P, TT, D], F32, yT_at + 32 * KIB)
    o_inv = at("o_inv", [P, S], F32, region + 33 * KIB)
    merged = at("merged", [P, KT, S], F32, region)
    g_tanh = at("g_tanh", [P, 4, S], F32, region + 32 * KIB)
    x_res = at("x_res", [P, TT, D], F32, region)
    junk = at("junk", [P, CH], F32, region + 32 * KIB)
    pg_tanh = at("pg_tanh", [P, TT, CH], F32, region + 32 * KIB)
    ple = at("ple", [P, TT, D], F32, hT_at)
    gfin = at("gfin", [P, D], F32, hT_at + 32 * KIB)
    junk2 = at("junk2", [P, CH], F32, hT_at + 40 * KIB)

    with ExitStack() as ctx:
        bank = [ctx.enter_context(nc.psum_tensor(f"bank{i}", [P, CH], F32)) for i in range(8)]

        def sem(name):
            return ctx.enter_context(nc.semaphore(name))

        ident_landed, p_landed, x_landed = sem("ident_landed"), sem("p_landed"), [sem(f"x_landed{t}") for t in range(TT)]
        small_landed, rel_landed = sem("small_landed"), sem("rel_landed")
        sq_done, rms_done, inv_done, scaled = sem("sq_done"), sem("rms_done"), sem("inv_done"), sem("scaled")
        ones_set = sem("ones_set")
        bias_mm, bias_added, bias_stored, bias_spread = sem("bias_mm"), sem("bias_added"), sem("bias_stored"), sem("bias_spread")
        p_turned, p_hi, p_lo = sem("p_turned"), sem("p_hi"), sem("p_lo")
        x_turned, h_hi, h_lo = sem("x_turned"), sem("h_hi"), sem("h_lo")
        raw_landed = [sem(f"raw_landed{i}") for i in range(RAW)]
        hi_ready, lo_ready, step_done = sem("hi_ready"), sem("lo_ready"), sem("step_done")
        acc_done = sem("acc_done")
        bank_read = [sem(f"bank_read{j}") for j in range(4)]
        merge_read = [sem(f"merge_read{j}") for j in range(4)]
        v_turned, v_nat_ready = sem("v_turned"), sem("v_nat_ready")
        k_summed, k_mean_ready = sem("k_summed"), sem("k_mean_ready")
        scores_done, gate_finite, cap_ready = sem("scores_done"), sem("gate_finite"), sem("cap_ready")
        biased, max_ready, exp_done = sem("biased"), sem("max_ready"), sem("exp_done")
        inv_ready, probs_ready = sem("inv_ready"), sem("probs_ready")
        p_turn, pT_act, pT_dve = sem("p_turn"), sem("pT_act"), sem("pT_dve")
        zs_ready, table_landed, rot_landed = sem("zs_ready"), sem("table_landed"), sem("rot_landed")
        rot_cos_done, rot_sin_done, rotated = sem("rot_cos_done"), sem("rot_sin_done"), sem("rotated")
        pv_done, osq_ready, mean_done, root_ready = sem("pv_done"), sem("osq_ready"), sem("mean_done"), sem("root_ready")
        oinv_ready, gated, y_ready, y_hi, y_lo = sem("oinv_ready"), sem("gated"), sem("y_ready"), sem("y_hi"), sem("y_lo")
        merged_ready, tanh_ready = sem("merged_ready"), sem("tanh_ready")
        m_hi, m_lo = sem("m_hi"), sem("m_lo")
        xres_landed, x1_sq = sem("xres_landed"), sem("x1_sq")
        ple_stored, ple_landed = sem("ple_stored"), sem("ple_landed")
        x1_turned, hp_hi, hp_lo = sem("x1_turned"), sem("hp_hi"), sem("hp_lo")
        sum1_ready, rms1_ready, inv1_ready, half1_ready = sem("sum1_ready"), sem("rms1_ready"), sem("inv1_ready"), sem("half1_ready")
        gfin_landed, pg_added, x2_ready, x2_sq = sem("gfin_landed"), sem("pg_added"), sem("x2_ready"), sem("x2_sq")
        x2_scaled = sem("x2_scaled")
        sum2_ready, rms2_ready, inv2_ready = sem("sum2_ready"), sem("rms2_ready"), sem("inv2_ready")
        out_ready, last_ready, out_stored = sem("out_ready"), sem("last_ready"), sem("out_stored")

        block = ctx.enter_context(nc.Block())

        def wait_sums(eng, j, group, last_step):
            if j < 3:
                eng.wait_ge(acc_done, group * 3 + (j + 1))
            else:
                eng.wait_ge(step_done, last_step + 1)

        def wait_last_sums(eng, t):
            if t % 2 == 0:
                eng.wait_ge(acc_done, 3 * (G_GATE + NC_ - 1) + t // 2 + 1)
            else:
                eng.wait_ge(step_done, LAST0 + (t // 2 + 1) * KT)

        G_HEAD = NC_
        G_MERGE = G_HEAD + 2 * NH
        G_OUT = G_MERGE + 4 * NC_
        G_GATE = G_OUT + NC_
        R_HEAD = NC_
        R_MERGE = R_HEAD + 2 * NH
        R_OUT = R_MERGE + 2 * NC_
        R_GATE = R_OUT + NC_

        def score_at(t):
            return P * (t * (t + 1) // 2)

        def decayed_at(t):
            return P * (t * TT - t * (t - 1) // 2)

        @block.sync
        def _(sp):
            sp.dma_start(ident[:, :], c_ident).then_inc(ident_landed, 16)
            sp.dma_start(p_nat[:, :, :], p2d.rearrange("(t p) d -> p t d", p=P)).then_inc(p_landed, 16)
            def vectors():
                with nc.allow_non_contiguous_dma(reason="two [2048] vectors, once"):
                    sp.dma_start(gmix_col[:, :], g_mix.rearrange("l (c p) -> p (l c)", p=P)).then_inc(small_landed, 16)
                    sp.dma_start(gple_col[:, :], g_ple.rearrange("l (c p) -> p (l c)", p=P)).then_inc(small_landed, 16)
                sp.dma_start(rel_sb[:, :], rel_bias).then_inc(rel_landed, 16)
                sp.dma_start(onehot[:, :], c_onehot).then_inc(rel_landed, 16)
                sp.dma_start(mask_row[:, :], c_mask).then_inc(rel_landed, 16)

            def load(step_mod, step, src, waits=True, pairs=False):
                slot = step_mod % RAW
                if waits:
                    sp.wait_ge(lo_ready, step - (RAW - 1))
                dst = raw[:, slot, :].rearrange("p (t c) -> p t c", c=src.shape[-1])
                if pairs:
                    src = src.rearrange("(c two) t n -> two c (t n)", two=2)
                    dst = raw[:, slot, :]
                sp.dma_start(dst, src).then_inc(raw_landed[slot], 16)

            def head_weights(k, family, h):
                cols = W_in[k * P:(k + 1) * P, family * 4 * D_A:(family + 1) * 4 * D_A]
                return cols.rearrange("p (t c) -> p t c", t=4)[:, :, bass.ds(h * DH, DH)]

            def weights(W, k, n):
                return W[k * P:(k + 1) * P, bass.ds(n * CH, CH)].rearrange("p (t c) -> p t c", t=1)

            for n in range(NC_):
                for k in range(KP):
                    load(KP * n + k, KP * n + k, weights(W_pp, k, n), waits=False)
            for t in range(TT):
                sp.dma_start(x_nat[:, t, :], x2d[t * P:(t + 1) * P, :]).then_inc(x_landed[t], 16)
            vectors()
            for k in range(KT):
                load(k, HEAD0 + k, head_weights(k, 0, 0))
            sp.wait_ge(bias_added, 2)
            sp.dma_start(bias_row[:, :], bias_vec[:, :]).then_inc(bias_stored, 16)
            sp.wait_ge(bias_stored, 16)
            sp.dma_start(bias_rep[0:NH * P * REV].rearrange("(h i r) -> h i r", h=NH, i=P),
                         bias_row[:, :].rearrange("h (i r) -> h i r", i=1).to_broadcast([NH, P, REV])
                         ).then_inc(bias_spread, 16)

            def bias_table(h):
                first = bias_rep[bass.ds(h * (P * REV) + (P - 1), P * (REV - 1))]
                return first.rearrange("(i r) -> i r", r=REV - 1)[:, 0:S]

            with sp.Fori(1, NH) as h:
                for k in range(KT):
                    load(k, h * KT + (HEAD0 + k), head_weights(k, 0, h))
                    if k == 2:
                        sp.wait_ge(x_turned, KT)
                        sp.wait_ge(bias_spread, 16)
                        sp.dma_start(table[:, :], bias_table(h - 1)).then_inc(table_landed, 16)
            for k in range(KT):
                load(k, HEAD0 + NH * KT + k, head_weights(k, 1, 0))
                if k == 0:
                    sp.wait_ge(probs_ready, TT * (NH - 1))
                    sp.dma_start(table[:, :], bias_table(NH - 1)).then_inc(table_landed, 16)
                    sp.dma_start(cos_sb[:, :], c_cos).then_inc(rot_landed, 16)
                    sp.dma_start(sin_sb[:, :], c_sin).then_inc(rot_landed, 16)
            with sp.Fori(1, NH) as h:
                for k in range(KT):
                    load(k, h * KT + (HEAD0 + NH * KT + k), head_weights(k, 1, h))
                    if k == 0:
                        sp.wait_ge(probs_ready, h * TT + TT * (NH - 1))
                        sp.dma_start(table[:, :], c_decay[bass.ds(h - 1, 1), :, :].rearrange("h p c -> (h p) c")
                                     ).then_inc(table_landed, 16)

            def merge_loads(n, base, last_table):
                for k in range(KT):
                    ahead = 1 if k == KT - 1 else 0
                    sp.wait_ge(lo_ready, base + (k + ahead - (RAW - 1)))
                    load(k, base + k, weights(W_in[:, GATES:GATES + D], k, n), waits=False)
                    if last_table and k == 0:
                        sp.wait_ge(probs_ready, TT * (2 * NH - 1))
                        sp.dma_start(table[:, :], c_decay[NH - 1]).then_inc(table_landed, 16)
                for k in range(KY):
                    load(k, base + (KT + k), weights(W_a, k, n), waits=k > 0)
                for k in range(KT):
                    load(k, base + (KT + KY + k), weights(W_in[:, GATES + D:GATES + 2 * D], k, n))
                for k in range(KY):
                    load(k, base + (2 * KT + KY + k), weights(W_b, k, n), pairs=True)

            merge_loads(0, MERGE0, True)
            with sp.Fori(1, NC_) as n:
                merge_loads(n, n * MERGE_STEPS + MERGE0, False)
            with sp.Fori(0, NC_) as n:
                for k in range(KT):
                    load(k, n * KT + (OUT0 + k), weights(W_out, k, n))
            for k in range(KT):
                load(k, GATE0 + k, weights(W_pg, k, 0))
            sp.wait_ge(step_done, GATE0)
            sp.wait_ge(ple_stored, 16 * NC_)
            for t in range(TT):
                sp.dma_start(ple[:, t, :], ple_kept[t * P:(t + 1) * P, :]).then_inc(ple_landed, 16)
            sp.dma_start(gfin[:, :], g_final.rearrange("(o d) -> o d", o=1).to_broadcast([P, D])
                         ).then_inc(gfin_landed, 16)
            with sp.Fori(1, NC_ - 1) as n:
                for k in range(KT):
                    load(k, n * KT + (GATE0 + k), weights(W_pg, k, n))
            for half in range(2):
                for k in range(KT):
                    load(k, LAST0 + half * KT + k, weights(W_pg, k, NC_ - 1))
            for t in range(TT):
                own = D - CH if t < TT - 1 else D - 2 * CH
                sp.wait_ge(out_ready, t + 1)
                sp.dma_start(out2d[t * P:(t + 1) * P, 0:own], x_res[:, t, 0:own]).then_inc(out_stored, 16)
                sp.wait_ge(last_ready, t + 1 + (t == TT - 1))
                sp.dma_start(out2d[t * P:(t + 1) * P, own:], x_res[:, t, own:]).then_inc(out_stored, 16)
            sp.wait_ge(out_stored, 2 * 16 * TT)

        @block.tensor
        def _(pe):
            def passes(acc, st_hi, st_lo, mv_hi, mv_lo, first, last):
                pe.matmul(acc, st_hi, mv_hi, start=first, stop=False)
                pe.matmul(acc, st_hi, mv_lo, start=False, stop=False)
                return pe.matmul(acc, st_lo, mv_hi, start=False, stop=last)

            def parts_ready(step):
                pe.wait_ge(hi_ready, step + 1)
                pe.wait_ge(lo_ready, step + 1)

            def transposed_step(step_mod, step, accs, a_hi, a_lo, first, last, free=None):
                slot = step_mod % SPLIT
                parts_ready(step)
                for j in range(4):
                    if first and free is not None:
                        free(j)
                    hi, lo = w_hi[:, slot, j * P:(j + 1) * P], w_lo[:, slot, j * P:(j + 1) * P]
                    mm = passes(accs[j][:, :], hi, lo, a_hi, a_lo, first, last)
                    if last and j < 3:
                        mm.then_inc(acc_done, 1)
                mm.then_inc(step_done, 1)

            def natural_step(step_mod, step, accs, a_hi, a_lo, first, last, free=None, tiles=range(TT)):
                slot = step_mod % SPLIT
                parts_ready(step)
                for t in tiles:
                    if first and free is not None:
                        free(t)
                    mm = passes(accs[t][:, :], a_hi[:, t * P:(t + 1) * P], a_lo[:, t * P:(t + 1) * P],
                                w_hi[:, slot, :], w_lo[:, slot, :], first, last)
                    if last and t != tiles[-1]:
                        mm.then_inc(acc_done, 1)
                mm.then_inc(step_done, 1)

            low, high = bank[0:4], bank[4:8]

            pe.wait_ge(ident_landed, 16)
            pe.wait_ge(p_landed, 16)
            for c in range(KP):
                for t in range(TT):
                    mm = pe.transpose(bank[6 + c][:, t * P:(t + 1) * P], p_nat[:, t, c * P:(c + 1) * P], ident[:, :])
                mm.then_inc(p_turned, 1)
            for n in range(NC_):
                for k in range(KP):
                    if n == 0:
                        pe.wait_ge(p_hi, k + 1)
                        pe.wait_ge(p_lo, k + 1)
                    step = n * KP + k
                    natural_step(step, step, low, pT_hi[:, k, :], pT_lo[:, k, :], k == 0, k == KP - 1,
                                 lambda t: pe.wait_ge(bank_read[t], n) if n else None)
            pe.wait_ge(rel_landed, 48)
            for i in range(2):
                half = slice(i * REV // 2, (i + 1) * REV // 2)
                pe.matmul(bank[4 + i][0:NH, 0:REV // 2], rel_sb[:, :], onehot[:, half],
                          start=True, stop=True).then_inc(bias_mm, 1)

            def turn_x(c):
                if c >= 4:
                    pe.wait_ge(h_lo, c - 3)
                elif c < 2:
                    pe.wait_ge(bias_added, c + 1)
                for t in range(TT):
                    if c == 0:
                        pe.wait_ge(scaled, t + 1)
                    mm = pe.transpose(high[c % 4][:, t * P:(t + 1) * P], x_nat[:, t, c * P:(c + 1) * P], ident[:, :])
                mm.then_inc(x_turned, 1)

            def values_turned(J):
                pe.wait_ge(bank_read[2], J + (R_HEAD + 1))
                for t in range(TT):
                    mm = pe.transpose(high[3][:, t * P:(t + 1) * P], v_sb[:, t * P:(t + 1) * P], ident[:, :])
                mm.then_inc(v_turned, 1)

            def attention(k, J):
                if k == 0:
                    pe.wait_ge(y_ready, J + 1)
                    values_turned(J)
                if k == 1:
                    pe.wait_ge(bank_read[0], J + (R_HEAD + 1))
                    pe.wait_ge(bank_read[1], J + (R_HEAD + 1))
                    pe.wait_ge(k_mean_ready, J + 1)
                    for i in range(2):
                        pe.matmul(high[0][:, CH - 2 + i:CH - 1 + i], q_sb[:, (2 + i) * P:(3 + i) * P], k_mean[:, :],
                                  start=True, stop=True)
                    for t in range(3):
                        pe.matmul(high[t][:, 0:(t + 1) * P], q_sb[:, t * P:(t + 1) * P], k_sb[:, 0:(t + 1) * P],
                                  start=True, stop=True).then_inc(scores_done, 1)
                if k == 2:
                    pe.wait_ge(v_nat_ready, J + 1)
                    pe.matmul(high[3][:, :], q_sb[:, 3 * P:4 * P], k_sb[:, :],
                              start=True, stop=True).then_inc(scores_done, 1)
                for t, at_k in enumerate((7, 8, 9, 10)):
                    if k == at_k:
                        pe.wait_ge(probs_ready, J * TT + (t + 1))
                        for kt in range(t + 1):
                            a = score_at(t) + kt * P
                            mm = pe.transpose(high[t][:, kt * P:(kt + 1) * P], probs[:, a:a + P], ident[:, :])
                        mm.then_inc(p_turn, 1)
                if k == 12:
                    pe.wait_ge(pT_act, J * 2 + 2)
                    pe.wait_ge(pT_dve, J * 2 + 2)
                    for kt in range(TT):
                        mm = pe.matmul(high[0][:, kt * P:], v_nat[:, kt, :], probsT[:, kt, kt * P:],
                                       start=(kt == 0), stop=(kt == TT - 1))
                    mm.then_inc(pv_done, 1)

            def retention(k, J):
                if k == 0:
                    pe.wait_ge(y_ready, J + 1)
                    values_turned(J)
                if k == 3:
                    pe.wait_ge(rotated, (J - NH) * 2 + 3)
                    pe.wait_ge(v_nat_ready, J + 1)
                    for kt in range(TT):
                        pe.matmul(high[kt][:, 0:S - kt * P], k_sb[:, kt * P:(kt + 1) * P], q_sb[:, kt * P:],
                                  start=True, stop=True).then_inc(scores_done, 1)
                if k == 8:
                    pe.wait_ge(probs_ready, J * TT + TT)
                    for kt in range(TT):
                        a = decayed_at(kt)
                        mm = pe.matmul(high[0][:, kt * P:], v_nat[:, kt, :], probs[:, a:a + S - kt * P],
                                       start=(kt == 0), stop=(kt == TT - 1))
                    mm.then_inc(pv_done, 1)
                if k == 10:
                    pe.wait_ge(osq_ready, J - NH + 1)
                    pe.matmul(high[1][:, :], ones[:, :], o_sq[:, :], start=True, stop=True).then_inc(mean_done, 1)

            def head_group(G, job):
                def free(j):
                    pe.wait_ge(bank_read[j], G + R_HEAD)
                for k in range(KT):
                    if isinstance(G, int) and G == 0:
                        pe.wait_ge(h_hi, k + 1)
                        pe.wait_ge(h_lo, k + 1)
                    transposed_step(k, G * KT + (HEAD0 + k), low, hT_hi[:, k, :], hT_lo[:, k, :], k == 0, k == KT - 1,
                                         free)
                    job(k)

            for c in range(4):
                turn_x(c)
            head_group(0, lambda k: turn_x(k + 4) if k + 4 < KT else None)
            with pe.Fori(1, NH) as h:
                head_group(h, lambda k: attention(k, h - 1))
            head_group(NH, lambda k: attention(k, NH - 1))
            with pe.Fori(NH + 1, 2 * NH) as G:
                head_group(G, lambda k: retention(k, G - 1))

            def merge_group(n, base, job):
                def free_low(g):
                    return lambda j: pe.wait_ge(bank_read[j], g)

                def free_high(g, always):
                    return lambda j: pe.wait_ge(merge_read[j], g) if always else None
                for k in range(KT):
                    transposed_step(k, base + k, low, hT_hi[:, k, :], hT_lo[:, k, :], k == 0, k == KT - 1,
                                         free_low(2 * n + R_MERGE))
                    job(k)
                first_chunk = isinstance(n, int) and n == 0
                for k in range(KY):
                    if first_chunk and k == 0:
                        pe.wait_ge(y_hi, NH)
                        pe.wait_ge(y_lo, NH)
                        pe.wait_ge(y_ready, 2 * NH + 1)
                    transposed_step(k, base + (KT + k), high, yT_hi[:, k, :], yT_lo[:, k, :], k == 0, k == KY - 1,
                                         free_high(2 * n, not first_chunk))
                for k in range(KT):
                    transposed_step(k, base + (KT + KY + k), low, hT_hi[:, k, :], hT_lo[:, k, :], k == 0,
                                         k == KT - 1, free_low(2 * n + (R_MERGE + 1)))
                for k in range(KY):
                    if first_chunk and k == 0:
                        pe.wait_ge(y_hi, 2 * NH)
                        pe.wait_ge(y_lo, 2 * NH)
                    transposed_step(k, base + (2 * KT + KY + k), high, yT_hi[:, KY + k, :], yT_lo[:, KY + k, :],
                                         k == 0, k == KY - 1, free_high(2 * n + 1, True))

            merge_group(0, MERGE0, lambda k: retention(k, 2 * NH - 1))
            with pe.Fori(1, NC_) as n:
                merge_group(n, n * MERGE_STEPS + MERGE0, lambda k: None)

            def turn_x1(n, i):
                for t in range(TT):
                    pe.wait_ge(bank_read[t], R_OUT + n + 1)
                if n == 0:
                    pe.wait_ge(merge_read[i], 2 * NC_)
                else:
                    pe.wait_ge(hp_lo, n * 4 + (i - 3))
                for t in range(TT):
                    mm = pe.transpose(high[i][:, t * P:(t + 1) * P],
                                      x_res[:, t, n * CH + i * P:n * CH + (i + 1) * P], ident[:, :])
                mm.then_inc(x1_turned, 1)

            def out_chunk(n, job):
                def free(t):
                    pe.wait_ge(bank_read[t], R_OUT + n)
                for k in range(KT):
                    if isinstance(n, int) and n == 0:
                        pe.wait_ge(m_hi, k + 1)
                        pe.wait_ge(m_lo, k + 1)
                    natural_step(k, n * KT + (OUT0 + k), low, hT_hi[:, k, :], hT_lo[:, k, :],
                                      k == 0, k == KT - 1, free)
                    job(k)

            out_chunk(0, lambda k: None)
            for n in range(1, NC_):
                out_chunk(n, lambda k: turn_x1(n - 1, (k - 3) // 3) if k in (3, 6, 9, 12) else None)

            def gate_chunk(n):
                def free(t):
                    pe.wait_ge(bank_read[t], n + R_GATE)
                for k in range(KT):
                    if isinstance(n, int) and n == 0:
                        pe.wait_ge(hp_hi, k + 1)
                        pe.wait_ge(hp_lo, k + 1)
                    natural_step(k, n * KT + (GATE0 + k), low, yT_hi[:, k, :], yT_lo[:, k, :],
                                 k == 0, k == KT - 1, free)
                    if isinstance(n, int) and n == 0 and k in (3, 6, 9, 12):
                        turn_x1(NC_ - 1, (k - 3) // 3)

            gate_chunk(0)
            with pe.Fori(1, NC_ - 1) as n:
                gate_chunk(n)
            for half in range(2):
                tiles = (2 * half, 2 * half + 1)
                for k in range(KT - SPLIT * half):
                    natural_step(k, LAST0 + half * KT + k, low, yT_hi[:, k, :], yT_lo[:, k, :], k == 0, k == KT - 1,
                                 lambda t: pe.wait_ge(bank_read[t], NC_ - 1 + R_GATE), tiles)
            for t in tiles:
                for k in range(KT - SPLIT, KT):
                    if t == tiles[0]:
                        parts_ready(LAST0 + KT + k)
                    mm = passes(bank[t][:, :], yT_hi[:, k, t * P:(t + 1) * P], yT_lo[:, k, t * P:(t + 1) * P],
                                w_hi[:, k % SPLIT, :], w_lo[:, k % SPLIT, :], False, k == KT - 1)
                    if t == tiles[-1]:
                        mm.then_inc(step_done, 1)
                if t == tiles[0]:
                    mm.then_inc(acc_done, 1)

        def tile_landed(eng, mod, step):
            use = step // RAW * 16 if isinstance(step, int) else (step - mod) * (16 // RAW)
            eng.wait_ge(raw_landed[mod], use + 16)

        def parts_free(eng, step):
            if not (isinstance(step, int) and step < SPLIT):
                eng.wait_ge(step_done, step - (SPLIT - 1))

        def raw_view(tile, pairs):
            return tile.rearrange("p (j c two) -> p j two c", j=4, two=2) if pairs else tile

        def split_view(tile, pairs):
            return tile.rearrange("p (j two c) -> p j two c", j=4, two=2) if pairs else tile

        @block.scalar
        def _(act):
            def split_hi(mod, step, pairs=False):
                if isinstance(step, int) and step >= STEPS:
                    return
                mod = mod % RAW
                tile_landed(act, mod, step)
                parts_free(act, step)
                act.activation(split_view(w_hi[:, mod % SPLIT, :], pairs), raw_view(raw[:, mod, :], pairs), COPY
                               ).then_inc(hi_ready, 1)

            def x_rms(t):
                act.wait_ge(x_landed[t], 16)
                act.activation(sq_junk[:, :], x_nat[:, t, :], ACT.Square, accum_out=sq_x[:, t:t + 1]).then_inc(sq_done, 1)
                act.wait_ge(sq_done, t + 1)
                act.activation(rms_x[:, t:t + 1], sq_x[:, t:t + 1], ACT.Sqrt, bias=eps_col[:, :], scale=1.0 / D
                               ).then_inc(rms_done, 1)

            for c in range(KP):
                act.wait_ge(p_turned, c + 1)
                act.activation(pT_hi[:, c, :], bank[6 + c][:, :], COPY).then_inc(p_hi, 1)
            for k in range(LEAD):
                split_hi(k, k)
            act.wait_ge(ones_set, 2)
            for n in range(NC_):
                for k in range(KP):
                    step = n * KP + k
                    split_hi(step + LEAD, step + LEAD)
                if n == 1:
                    x_rms(1)
                for t in (0, 1):
                    wait_sums(act, t, n, None)
                    act.activation(ple_out[:, t, n * CH:(n + 1) * CH], bank[t][:, :], COPY, scale=0.5
                                   ).then_inc(bank_read[t], 1)
                if n == 0:
                    x_rms(0)
                if n == 1:
                    x_rms(2)
                if n == 2:
                    x_rms(3)
            for n in range(NC_):
                for t in range(TT):
                    act.wait_ge(bank_read[t], n + 1)
                act.dma_start(ple_kept[:, n * CH:(n + 1) * CH].rearrange("(t p) c -> p t c", p=P),
                              ple_out[:, :, n * CH:(n + 1) * CH]).then_inc(ple_stored, 16)

            def h_part(c):
                act.wait_ge(x_turned, c + 1)
                act.wait_ge(small_landed, 32)
                act.activation(hT_hi[:, c, :], bank[4 + c % 4][:, :], COPY, scale=gmix_col[:, c:c + 1]).then_inc(h_hi, 1)

            def attention(k, J):
                if k == 1:
                    act.wait_ge(v_turned, J + 1)
                    act.activation(v_nat[:, :, :].rearrange("p t d -> p (t d)"), bank[7][:, :], COPY).then_inc(v_nat_ready, 1)
                for t in range(TT):
                    if k == 3 + t:
                        act.wait_ge(max_ready, J * TT + (t + 1))
                        a, n = score_at(t), (t + 1) * P
                        act.activation(probs[:, a:a + n], probs[:, a:a + n], ACT.Exp, bias=neg_max[:, t:t + 1],
                                       accum_out=row_sum[:, t:t + 1]).then_inc(exp_done, 1)
                for t, at_k in ((0, 8), (2, 10)):
                    if k == at_k:
                        act.wait_ge(p_turn, J * TT + (t + 1))
                        act.activation(probsT[:, 0:t + 1, t * P:(t + 1) * P],
                                       bank[4 + t][:, 0:(t + 1) * P].rearrange("p (k q) -> p k q", q=P), COPY
                                       ).then_inc(pT_act, 1)
                y_part(k, J)

            def y_part(k, J):
                if k == 14:
                    act.wait_ge(y_ready, J + 2)
                    act.activation(yT_hi[:, bass.ds(J, 1), :].rearrange("p j s -> p (j s)"), y32[:, :], COPY).then_inc(y_hi, 1)

            def retention(k, J):
                if k == 1:
                    act.wait_ge(v_turned, J + 1)
                    act.activation(v_nat[:, :, :].rearrange("p t d -> p (t d)"), bank[7][:, :], COPY).then_inc(v_nat_ready, 1)
                if k == 9:
                    act.wait_ge(pv_done, J + 1)
                    act.activation(o_sq[:, :], bank[4][:, :], ACT.Square).then_inc(osq_ready, 1)
                if k == 11:
                    act.wait_ge(mean_done, J - (NH - 1))
                    act.activation(o_rms[:, :], bank[5][:, :], ACT.Sqrt, bias=eps_col[:, :]).then_inc(root_ready, 1)
                y_part(k, J)

            def head_group(G, job, pairs, next_pairs):
                first = isinstance(G, int) and G == 0
                for k in range(KT):
                    split_hi(k + LEAD, G * KT + (HEAD0 + k + LEAD), pairs if k + LEAD < KT else next_pairs)
                    job(k)
                wait_sums(act, 0, G + G_HEAD, None)
                if not first:
                    act.wait_ge(scores_done, G * TT)
                act.activation(q_sb[:, :], bank[0][:, :], COPY, scale=float(DH) ** -0.5).then_inc(bank_read[0], 1)
                wait_sums(act, 2, G + G_HEAD, None)
                if not first:
                    act.wait_ge(v_turned, G)
                act.activation(v_sb[:, :], bank[2][:, :], COPY).then_inc(bank_read[2], 1)
                act.wait_ge(bank_read[3], G + (R_HEAD + 1))
                if not first:
                    act.wait_ge(zs_ready, G)
                act.activation(z_tanh[:, :], z_half[:, :], ACT.Tanh).then_inc(tanh_ready, 1)

            for c in range(4):
                h_part(c)
            head_group(0, lambda k: h_part(k + 4) if k + 4 < KT else None, False, False)
            with act.Fori(1, NH - 1) as h:
                head_group(h, lambda k: attention(k, h - 1), False, False)
            head_group(NH - 1, lambda k: attention(k, NH - 2), False, True)
            head_group(NH, lambda k: attention(k, NH - 1), True, True)
            with act.Fori(NH + 1, 2 * NH - 1) as G:
                head_group(G, lambda k: retention(k, G - 1), True, True)
            head_group(2 * NH - 1, lambda k: retention(k, 2 * NH - 2), True, False)

            def merge_group(n, base, job):
                first_chunk = isinstance(n, int) and n == 0
                for k in range(KT):
                    split_hi(k + LEAD, base + (k + LEAD))
                    job(k)
                for j in range(4):
                    wait_sums(act, j, n * 4 + G_MERGE, base + (KT - 1))
                    if not first_chunk:
                        act.wait_ge(merged_ready, n * 4 + (j - 3))
                    act.activation(g_tanh[:, j, :], bank[j][:, :], ACT.Tanh, scale=0.5).then_inc(bank_read[j], 1)
                for k in range(KY + KT):
                    split_hi(k + LEAD, base + (KT + k + LEAD))
                for j in range(4):
                    wait_sums(act, j, n * 4 + (G_MERGE + 2), base + (2 * KT + KY - 1))
                    act.wait_ge(merge_read[j], n * 2 + 1)
                    act.activation(g_tanh[:, j, :], bank[j][:, :], ACT.Tanh, scale=0.5).then_inc(bank_read[j], 1)
                for k in range(KY):
                    split_hi(k + LEAD, base + (2 * KT + KY + k + LEAD))
                if isinstance(n, int) and n == NC_ - 1:
                    for c in range(4):
                        merged_part(c)

            merge_group(0, MERGE0, lambda k: retention(k, 2 * NH - 1))
            def merged_part(c):
                act.wait_ge(merged_ready, c + 1)
                if c == 0:
                    act.wait_ge(step_done, OUT0 - KY)
                act.activation(hT_hi[:, c, :], merged[:, c, :], COPY, scale=0.5).then_inc(m_hi, 1)

            def hp_part(c):
                act.wait_ge(x1_turned, c + 1)
                act.activation(yT_hi[:, c, :], bank[4 + c % 4][:, :], COPY, scale=gple_col[:, c:c + 1]).then_inc(hp_hi, 1)

            def x1_square(n, t):
                act.wait_ge(bank_read[t], R_OUT + n + 1)
                if n or t:
                    act.wait_ge(x1_sq, n * TT + t)
                act.activation(junk[:, :], x_res[:, t, n * CH:(n + 1) * CH], ACT.Square,
                               accum_out=sq1[:, t, n:n + 1]).then_inc(x1_sq, 1)

            with act.Fori(1, NC_ - 1) as n:
                merge_group(n, n * MERGE_STEPS + MERGE0, lambda k: None)
            merge_group(NC_ - 1, (NC_ - 1) * MERGE_STEPS + MERGE0, lambda k: None)
            for n in range(NC_):
                for k in range(KT):
                    split_hi(k + LEAD, OUT0 + n * KT + k + LEAD)
                    if n == 0:
                        for c in (4 + 2 * k, 5 + 2 * k):
                            if c < KT:
                                merged_part(c)
                        if k == 7:
                            act.wait_ge(m_lo, KT)
                            for t in range(TT):
                                act.dma_start(x_res[:, t, :], x2d[t * P:(t + 1) * P, :]).then_inc(xres_landed, 16)
                    else:
                        if k in (0, 1, 2, 3):
                            x1_square(n - 1, k)
                        if k in (4, 7, 10, 13):
                            hp_part((n - 1) * 4 + (k - 4) // 3)

            def x2_square(t, n):
                if t or not (isinstance(n, int) and n == 0):
                    act.wait_ge(x2_sq, n * TT + t)
                act.wait_ge(x2_ready, n * TT + (t + 1))
                act.activation(junk2[:, :], x_res[:, t, bass.ds(n * CH, CH)], ACT.Square,
                               accum_out=sq2[:, t, bass.ds(n, 1)]).then_inc(x2_sq, 1)

            def gate_chunk(n):
                first = isinstance(n, int) and n == 0
                for k in range(KT):
                    split_hi(k + LEAD, n * KT + (GATE0 + k + LEAD))
                    if first:
                        if k in (0, 1, 2, 3):
                            x1_square(NC_ - 1, k)
                        if k in (4, 7, 10, 13):
                            hp_part((NC_ - 1) * 4 + (k - 4) // 3)
                        if k == 6:
                            act.wait_ge(sum1_ready, 1)
                            act.activation(rms1[:, :], sum1[:, :], ACT.Sqrt, bias=eps_col[:, :], scale=1.0 / D
                                           ).then_inc(rms1_ready, 1)
                    elif k in (1, 4, 7, 10):
                        x2_square(k // 3, n - 1)
                for t in range(TT):
                    if first:
                        act.wait_ge(half1_ready, 1)
                    else:
                        act.wait_ge(x2_ready, n * TT + (t - 3))
                    wait_sums(act, t, n + G_GATE, n * KT + (GATE0 + KT - 1))
                    act.activation(pg_tanh[:, t, :], bank[t][:, :], ACT.Tanh, scale=half1[:, t:t + 1]
                                   ).then_inc(bank_read[t], 1)

            gate_chunk(0)
            with act.Fori(1, NC_ - 1) as n:
                gate_chunk(n)
            last = NC_ - 1

            def last_tanh(t):
                act.wait_ge(x2_ready, last * TT + t - 3)
                wait_last_sums(act, t)
                act.activation(pg_tanh[:, t, :], bank[t][:, :], ACT.Tanh, scale=half1[:, t:t + 1]
                               ).then_inc(bank_read[t], 1)

            def last_root(t):
                act.wait_ge(sum2_ready, t + 1)
                act.activation(rms2[:, t:t + 1], sum2[:, t:t + 1], ACT.Sqrt, bias=eps_col[:, :], scale=1.0 / D
                               ).then_inc(rms2_ready, 1)

            def last_scale(t):
                act.wait_ge(inv2_ready, t + 1)
                act.wait_ge(x2_scaled, last * TT)
                chunks = slice(0, (last if t < TT - 1 else last - 1) * CH)
                act.activation(x_res[:, t, chunks], x_res[:, t, chunks], COPY, scale=inv2[:, t:t + 1]
                               ).then_inc(out_ready, 1)

            for k in range(KT):
                split_hi(k + LEAD, LAST0 + k + LEAD)
                if k in (1, 4, 7, 10):
                    x2_square(k // 3, last - 1)
            for k in range(KT):
                split_hi(k + LEAD, LAST0 + KT + k + LEAD)
                if k < 2:
                    last_tanh(k)
                if k in (2, 3):
                    x2_square(k - 2, last)
                if k == 4:
                    last_root(0)
                    last_root(1)
                if k in (6, 8):
                    last_scale((k - 6) // 2)
                if k == 10:
                    act.activation(warm[:, 0:1], eps_col[:, :], ACT.Tanh)
            last_tanh(2)
            x2_square(2, last)
            last_tanh(3)
            act.activation(warm[:, 1:2], eps_col[:, :], ACT.Sqrt)
            last_root(2)
            x2_square(3, last)
            last_scale(2)
            last_root(3)
            last_scale(3)

        @block.vector
        def _(dve):
            def split_lo(mod, step, pairs=False):
                if isinstance(step, int) and step >= STEPS:
                    return
                mod = mod % RAW
                tile_landed(dve, mod, step)
                parts_free(dve, step)
                dve.wait_ge(hi_ready, step + 1)
                dve.tensor_tensor(split_view(w_lo[:, mod % SPLIT, :], pairs), raw_view(raw[:, mod, :], pairs),
                                  split_view(w_hi[:, mod % SPLIT, :].bitcast(F32), pairs),
                                  ALU.subtract).then_inc(lo_ready, 1)

            dve.memset(eps_col[:, :], EPS).then_inc(ones_set, 1)
            dve.memset(ones[:, :], 1.0 / P).then_inc(ones_set, 1)
            dve.memset(k_sum[:, :], 0.0).then_inc(y_ready, 1)
            dve.memset(k_mean[:, :], 0.0).then_inc(rotated, 1)
            def x_scale(t):
                dve.wait_ge(rms_done, t + 1)
                dve.reciprocal(inv_x[:, t:t + 1], rms_x[:, t:t + 1]).then_inc(inv_done, 1)
                dve.wait_ge(inv_done, t + 1)
                dve.tensor_scalar(x_nat[:, t, :], x_nat[:, t, :], inv_x[:, t:t + 1], None, ALU.mult).then_inc(scaled, 1)

            for c in range(KP):
                dve.wait_ge(p_hi, c + 1)
                dve.tensor_tensor(pT_lo[:, c, :], bank[6 + c][:, :], pT_hi[:, c, :].bitcast(F32), ALU.subtract
                                  ).then_inc(p_lo, 1)
            for k in range(LEAD):
                split_lo(k, k)
            for n in range(NC_):
                for k in range(KP):
                    split_lo(n * KP + k + LEAD, n * KP + k + LEAD)
                for t in (2, 3):
                    wait_sums(dve, t, n, n * KP + KP - 1)
                    dve.tensor_scalar(ple_out[:, t, n * CH:(n + 1) * CH], bank[t][:, :], 0.5, None, ALU.mult
                                      ).then_inc(bank_read[t], 1)
                if n == 1:
                    x_scale(0)
                if n == 2:
                    x_scale(1)
                    x_scale(2)
                    x_scale(3)
            for i in range(2):
                half = slice(i * REV // 2, (i + 1) * REV // 2)
                dve.wait_ge(bias_mm, i + 1)
                dve.tensor_tensor(bias_vec[:, half], bank[4 + i][0:NH, 0:REV // 2], mask_row[:, half], ALU.add
                                  ).then_inc(bias_added, 1)

            def h_part(c):
                dve.wait_ge(h_hi, c + 1)
                dve.scalar_tensor_tensor(out=hT_lo[:, c, :], in0=bank[4 + c % 4][:, :], scalar=gmix_col[:, c:c + 1],
                                         in1=hT_hi[:, c, :].bitcast(F32), op0=ALU.mult, op1=ALU.subtract
                                         ).then_inc(h_lo, 1)

            def silu(J):
                dve.wait_ge(tanh_ready, J + 1)
                dve.scalar_tensor_tensor(out=z_half[:, :], in0=z_tanh[:, :], scalar=1.0, in1=z_half[:, :],
                                         op0=ALU.add, op1=ALU.mult).then_inc(zs_ready, 1)

            def y_part(k, J):
                if k == 14:
                    dve.wait_ge(y_hi, J + 1)
                    dve.tensor_tensor(yT_lo[:, bass.ds(J, 1), :].rearrange("p j s -> p (j s)"), y32[:, :],
                                      yT_hi[:, bass.ds(J, 1), :].rearrange("p j s -> p (j s)").bitcast(F32),
                                      ALU.subtract).then_inc(y_lo, 1)

            def attention(k, J):
                if k == 0:
                    dve.wait_ge(bank_read[1], J + (R_HEAD + 1))
                    dve.tensor_reduce(k_sum[:, :], k_sb[:, 0:BLOCK], AX.X, ALU.add).then_inc(k_summed, 1)
                    dve.wait_ge(k_summed, J + 1)
                    dve.tensor_scalar(k_mean[:, :], k_sum[:, :], float(DH) ** 0.5 / BLOCK, None, ALU.mult
                                      ).then_inc(k_mean_ready, 1)
                    silu(J)
                if k == 2:
                    dve.wait_ge(scores_done, J * TT + 1)
                    dve.tensor_scalar(finite[:, :], bank[4][:, CH - 2:CH], 0.0, 0.0, ALU.mult, ALU.is_equal
                                      ).then_inc(gate_finite, 1)
                    dve.wait_ge(gate_finite, J + 1)
                    dve.tensor_scalar(cap[:, :], finite[:, :], 2 * BIG, -BIG, ALU.mult, ALU.add).then_inc(cap_ready, 1)
                for t in range(TT):
                    a, n = score_at(t), (t + 1) * P
                    tab = (TT - 1 - t) * P
                    if k == 2 + t:
                        dve.wait_ge(scores_done, J * TT + (t + 1))
                        dve.wait_ge(table_landed, J * 16 + 16)
                        past = BLOCK if t * P >= BLOCK else 0
                        if past:
                            dve.wait_ge(cap_ready, J + 1)
                            dve.scalar_tensor_tensor(out=probs[:, a:a + past], in0=bank[4 + t][:, 0:past],
                                                     scalar=cap[:, t - 2:t - 1], in1=table[:, tab:tab + past],
                                                     op0=ALU.min, op1=ALU.add).then_inc(biased, 1)
                        dve.tensor_tensor(probs[:, a + past:a + n], bank[4 + t][:, past:n], table[:, tab + past:tab + n],
                                          ALU.add).then_inc(biased, 1)
                        dve.wait_ge(biased, J * 6 + (1, 2, 4, 6)[t])
                        dve.tensor_reduce(neg_max[:, t:t + 1], probs[:, a:a + n], AX.X, ALU.max, negate=True
                                          ).then_inc(max_ready, 1)
                    if k == 4 + t:
                        dve.wait_ge(exp_done, J * TT + (t + 1))
                        dve.reciprocal(row_inv[:, t:t + 1], row_sum[:, t:t + 1]).then_inc(inv_ready, 1)
                        dve.wait_ge(inv_ready, J * TT + (t + 1))
                        dve.tensor_scalar(probs[:, a:a + n], probs[:, a:a + n], row_inv[:, t:t + 1], None, ALU.mult
                                          ).then_inc(probs_ready, 1)
                for t, at_k in ((1, 9), (3, 11)):
                    if k == at_k:
                        dve.wait_ge(p_turn, J * TT + (t + 1))
                        dve.tensor_copy(probsT[:, 0:t + 1, t * P:(t + 1) * P],
                                        bank[4 + t][:, 0:(t + 1) * P].rearrange("p (k q) -> p k q", q=P)
                                        ).then_inc(pT_dve, 1)
                if k == 13:
                    dve.wait_ge(pv_done, J + 1)
                    dve.tensor_tensor(y32[:, :], bank[4][:, :], z_half[:, :], ALU.mult).then_inc(y_ready, 1)
                y_part(k, J)

            def retention(k, J):
                b = J - NH
                if k == 0:
                    silu(J)
                    dve.wait_ge(rot_landed, 32)
                for i, src in enumerate((q_sb, k_sb)):
                    if k == i:
                        dve.wait_ge(bank_read[i], J + (R_HEAD + 1))
                        dve.wait_ge(rotated, b * 2 + (i + 1))
                        dve.tensor_tensor(rot_cos[:, :], src[:, :], cos_sb[:, :], ALU.mult).then_inc(rot_cos_done, 1)
                        for lo, hi in ((0, 64), (64, 0)):
                            dve.tensor_tensor(rot_sin[lo:lo + 64, :], src[hi:hi + 64, :], sin_sb[hi:hi + 64, :], ALU.mult
                                              ).then_inc(rot_sin_done, 1)
                        dve.wait_ge(rot_cos_done, b * 2 + (i + 1))
                        dve.wait_ge(rot_sin_done, b * 4 + (2 * i + 2))
                        dve.tensor_tensor(src[:, :], rot_cos[:, :], rot_sin[:, :], ALU.add).then_inc(rotated, 1)
                for kt in range(TT):
                    if k == 4 + kt // 2:
                        a, n = decayed_at(kt), S - kt * P
                        dve.wait_ge(scores_done, J * TT + (kt + 1))
                        dve.wait_ge(table_landed, J * 16 + 16)
                        dve.tensor_tensor(probs[:, a:a + n], bank[4 + kt][:, 0:n], table[:, 0:n], ALU.mult
                                          ).then_inc(probs_ready, 1)
                if k == 12:
                    dve.wait_ge(root_ready, b + 1)
                    dve.reciprocal(o_inv[:, :], o_rms[:, :]).then_inc(oinv_ready, 1)
                    dve.tensor_tensor(y32[:, :], bank[4][:, :], z_half[:, :], ALU.mult).then_inc(gated, 1)
                    dve.wait_ge(oinv_ready, b + 1)
                    dve.wait_ge(gated, b + 1)
                    dve.tensor_tensor(y32[:, :], y32[:, :], o_inv[:, :], ALU.mult).then_inc(y_ready, 1)
                y_part(k, J)

            def head_group(G, job, pairs, next_pairs):
                first = isinstance(G, int) and G == 0
                for k in range(KT):
                    split_lo(k + LEAD, G * KT + (HEAD0 + k + LEAD), pairs if k + LEAD < KT else next_pairs)
                    job(k)
                wait_sums(dve, 1, G + G_HEAD, None)
                if not first:
                    dve.wait_ge(scores_done, G * TT)
                dve.tensor_copy(k_sb[:, :], bank[1][:, :]).then_inc(bank_read[1], 1)
                wait_sums(dve, 3, G + G_HEAD, G * KT + (HEAD0 + KT - 1))
                dve.tensor_scalar(z_half[:, :], bank[3][:, :], 0.5, None, ALU.mult).then_inc(bank_read[3], 1)

            for c in range(4):
                h_part(c)
            head_group(0, lambda k: h_part(k + 4) if k + 4 < KT else None, False, False)
            dve.wait_ge(ple_stored, 16 * NC_)
            with dve.Fori(1, NH - 1) as h:
                head_group(h, lambda k: attention(k, h - 1), False, False)
            head_group(NH - 1, lambda k: attention(k, NH - 2), False, True)
            head_group(NH, lambda k: attention(k, NH - 1), True, True)
            with dve.Fori(NH + 1, 2 * NH - 1) as G:
                head_group(G, lambda k: retention(k, G - 1), True, True)
            head_group(2 * NH - 1, lambda k: retention(k, 2 * NH - 2), True, False)

            def merge_group(n, base, job):
                for k in range(KT):
                    split_lo(k + LEAD, base + (k + LEAD))
                    job(k)
                for k in range(KY):
                    split_lo(k + LEAD, base + (KT + k + LEAD))
                for j in range(4):
                    wait_sums(dve, j, n * 4 + (G_MERGE + 1), base + (KT + KY - 1))
                    dve.wait_ge(bank_read[j], n * 2 + (R_MERGE + 1))
                    dve.scalar_tensor_tensor(out=merged[:, bass.ds(n * 4 + j, 1), :].rearrange("p j s -> p (j s)"),
                                             in0=g_tanh[:, j, :], scalar=1.0, in1=bank[4 + j][:, :],
                                             op0=ALU.add, op1=ALU.mult).then_inc(merge_read[j], 1)
                for k in range(KT + KY):
                    split_lo(k + LEAD, base + (KT + KY + k + LEAD))
                if isinstance(n, int) and n == NC_ - 1:
                    for c in range(4):
                        merged_part(c)
                for j in range(4):
                    wait_sums(dve, j, n * 4 + (G_MERGE + 3), base + (MERGE_STEPS - 1))
                    dve.wait_ge(bank_read[j], n * 2 + (R_MERGE + 2))
                    dve.scalar_tensor_tensor(out=g_tanh[:, j, :], in0=g_tanh[:, j, :], scalar=1.0,
                                             in1=bank[4 + j][:, :], op0=ALU.add, op1=ALU.mult).then_inc(merge_read[j], 1)
                    dve.wait_ge(merge_read[j], n * 2 + 2)
                    tile = merged[:, bass.ds(n * 4 + j, 1), :].rearrange("p j s -> p (j s)")
                    dve.tensor_tensor(tile, tile, g_tanh[:, j, :], ALU.add).then_inc(merged_ready, 1)

            merge_group(0, MERGE0, lambda k: retention(k, 2 * NH - 1))
            def merged_part(c):
                dve.wait_ge(m_hi, c + 1)
                dve.scalar_tensor_tensor(out=hT_lo[:, c, :], in0=merged[:, c, :], scalar=0.5,
                                         in1=hT_hi[:, c, :].bitcast(F32), op0=ALU.mult, op1=ALU.subtract
                                         ).then_inc(m_lo, 1)

            def hp_part(c):
                dve.wait_ge(hp_hi, c + 1)
                dve.scalar_tensor_tensor(out=yT_lo[:, c, :], in0=bank[4 + c % 4][:, :], scalar=gple_col[:, c:c + 1],
                                         in1=yT_hi[:, c, :].bitcast(F32), op0=ALU.mult, op1=ALU.subtract
                                         ).then_inc(hp_lo, 1)

            with dve.Fori(1, NC_ - 1) as n:
                merge_group(n, n * MERGE_STEPS + MERGE0, lambda k: None)
            merge_group(NC_ - 1, (NC_ - 1) * MERGE_STEPS + MERGE0, lambda k: None)
            for n in range(NC_):
                for k in range(KT):
                    split_lo(k + LEAD, OUT0 + n * KT + k + LEAD)
                    if n == 0:
                        for c in (4 + 2 * k, 5 + 2 * k):
                            if c < KT:
                                merged_part(c)
                    elif k in (4, 7, 10, 13):
                        hp_part((n - 1) * 4 + (k - 4) // 3)
                if n == 0:
                    dve.wait_ge(xres_landed, 16 * TT)
                for t in range(TT):
                    wait_sums(dve, t, G_OUT + n, OUT0 + n * KT + KT - 1)
                    chunk = x_res[:, t, n * CH:(n + 1) * CH]
                    dve.tensor_tensor(chunk, bank[t][:, :], chunk, ALU.add).then_inc(bank_read[t], 1)

            def x2_times_g(t, n):
                dve.wait_ge(x2_sq, n * TT + (t + 1))
                chunk = x_res[:, t, bass.ds(n * CH, CH)]
                dve.tensor_tensor(chunk, chunk, gfin[:, bass.ds(n * CH, CH)], ALU.mult).then_inc(x2_scaled, 1)

            def x2(t, n):
                dve.wait_ge(bank_read[t], n + (R_GATE + 1))
                dve.scalar_tensor_tensor(out=pg_tanh[:, t, :], in0=pg_tanh[:, t, :], scalar=1.0,
                                         in1=ple[:, t, bass.ds(n * CH, CH)], op0=ALU.add, op1=ALU.mult
                                         ).then_inc(pg_added, 1)
                dve.wait_ge(pg_added, n * TT + (t + 1))
                chunk = x_res[:, t, bass.ds(n * CH, CH)]
                dve.tensor_tensor(chunk, chunk, pg_tanh[:, t, :], ALU.add).then_inc(x2_ready, 1)

            def gate_chunk(n):
                first = isinstance(n, int) and n == 0
                for k in range(KT):
                    split_lo(k + LEAD, n * KT + (GATE0 + k + LEAD))
                    if first:
                        if k in (4, 7, 10, 13):
                            hp_part((NC_ - 1) * 4 + (k - 4) // 3)
                        if k == 5:
                            dve.wait_ge(x1_sq, NC_ * TT)
                            dve.tensor_reduce(sum1[:, :], sq1[:, :, :], AX.X, ALU.add).then_inc(sum1_ready, 1)
                        if k == 8:
                            dve.wait_ge(rms1_ready, 1)
                            dve.reciprocal(inv1[:, :], rms1[:, :]).then_inc(inv1_ready, 1)
                            dve.wait_ge(inv1_ready, 1)
                            dve.tensor_scalar(half1[:, :], inv1[:, :], 0.5, None, ALU.mult).then_inc(half1_ready, 1)
                    else:
                        x2_of_chunk(k, n - 1)

            def x2_of_chunk(k, n):
                if k in (0, 3, 6, 9):
                    x2(k // 3, n)
                if k in (2, 5, 8, 11):
                    x2_times_g(k // 3, n)

            gate_chunk(0)
            dve.wait_ge(ple_landed, 16 * TT)
            dve.wait_ge(gfin_landed, 16)
            with dve.Fori(1, NC_ - 1) as n:
                gate_chunk(n)
            last = NC_ - 1

            def last_sum(t):
                dve.wait_ge(x2_sq, last * TT + t + 1)
                dve.tensor_reduce(sum2[:, t:t + 1], sq2[:, t, :], AX.X, ALU.add).then_inc(sum2_ready, 1)

            def last_inv(t):
                dve.wait_ge(rms2_ready, t + 1)
                dve.reciprocal(inv2[:, t:t + 1], rms2[:, t:t + 1]).then_inc(inv2_ready, 1)

            def last_scale(t):
                dve.wait_ge(inv2_ready, t + 1)
                if t == TT - 1:
                    chunk = x_res[:, t, (last - 1) * CH:last * CH]
                    dve.tensor_scalar(chunk, chunk, inv2[:, t:t + 1], None, ALU.mult).then_inc(last_ready, 1)
                dve.scalar_tensor_tensor(out=x_res[:, t, last * CH:], in0=x_res[:, t, last * CH:], scalar=inv2[:, t:t + 1],
                                         in1=gfin[:, last * CH:], op0=ALU.mult, op1=ALU.mult).then_inc(last_ready, 1)

            for k in range(KT):
                split_lo(k + LEAD, LAST0 + k + LEAD)
                x2_of_chunk(k, last - 1)
            for k in range(KT):
                split_lo(k + LEAD, LAST0 + KT + k + LEAD)
                if k in (1, 2):
                    x2(k - 1, last)
                if k in (3, 4):
                    last_sum(k - 3)
                if k == 5:
                    last_inv(0)
                    last_inv(1)
                if k in (6, 8):
                    last_scale((k - 6) // 2)
            x2(2, last)
            last_sum(2)
            x2(3, last)
            last_inv(2)
            last_scale(2)
            last_sum(3)
            last_inv(3)
            last_scale(3)


INPUTS = ["x", "p", "g_mix", "w_in", "w_a", "w_b", "w_out", "g_ple", "w_ple_gate", "w_ple_proj", "rel_bias",
          "g_final"]


def kernel(**inputs):
    import concourse.bacc as bacc
    from concourse.bass_utils import run_bass_kernel_spmd

    nc = bacc.Bacc("TRN2", target_bir_lowering=False, num_devices=1, dynamic_dma_scratch_size=2048)
    given = {name: np.ascontiguousarray(inputs[name]) for name in INPUTS}
    given.update(shape_constants())
    arrays, args = {}, {}
    for name, a in given.items():
        arrays[f"in_{name}"] = a
        args[name] = nc.dram_tensor(f"in_{name}", a.shape, mybir.dt.from_np(a.dtype), kind="ExternalInput").ap()
    out = nc.dram_tensor("out", inputs["x"].shape, F32, kind="ExternalOutput").ap()
    hybrid_block(nc, out=out, **args)
    result = run_bass_kernel_spmd(nc, [arrays], core_ids=[0])
    return result.results[0]["out"]
```

```python
from contextlib import ExitStack

import numpy as np
import concourse.bass as bass
from concourse import mybir

P = 128
S, D = 512, 2048
NH, DH = 8, 128
D_A = NH * DH
D_PLE = 256
EPS = 1e-6
BUCKETS, MAX_DISTANCE = 32, 128
BLOCK = 256
ROT_BASE = 10000.0

CH = 512
KT = D // P
KY = D_A // P
TT = S // P
NC_ = D // CH
RAW = 8
SPLIT = 4
LEAD = SPLIT - 1
GATES = 4 * D_A * 2
REV = 640
MASK = -1.0e30
BIG = 1.0e38

KP = D_PLE // P
HEAD0 = NC_ * KP
MERGE0 = HEAD0 + 2 * NH * KT
MERGE_STEPS = 2 * (KT + KY)
OUT0 = MERGE0 + NC_ * MERGE_STEPS
GATE0 = OUT0 + NC_ * KT
LAST0 = GATE0 + (NC_ - 1) * KT
STEPS = LAST0 + 2 * KT

F32, F32R = mybir.dt.float32, mybir.dt.float32r
ACT = mybir.ActivationFunctionType
ALU = mybir.AluOpType
AX = mybir.AxisListType
COPY = ACT.Copy


def shape_constants():
    f = np.float32
    dist = 511 - np.arange(REV)
    n = np.maximum(dist, 0)
    exact = BUCKETS // 2
    large = exact + (np.log(np.maximum(n, 1).astype(f) / f(exact)) / f(np.log(MAX_DISTANCE / exact))
                     * f(BUCKETS - exact)).astype(np.int32)
    bucket = np.where(n < exact, n, np.minimum(large, BUCKETS - 1))
    onehot = ((np.arange(BUCKETS)[:, None] == bucket[None]) & (dist >= 0)[None]).astype(f)
    mask = np.broadcast_to(np.where(dist >= 0, f(0), f(MASK)), (NH, REV)).astype(f)
    theta = (f(1) / (f(ROT_BASE) ** np.linspace(0, 1, DH // 2, dtype=f))).astype(f)
    ang = (np.arange(S, dtype=f)[:, None] * theta[None]).astype(f).T
    cos, sin = np.cos(ang).astype(f), np.sin(ang).astype(f)
    gamma = 1.0 - 2.0 ** (-5.0 - np.arange(NH))
    diff = np.arange(S)[None, :] - np.arange(P)[:, None]
    decay = np.where(diff >= 0, gamma[:, None, None] ** np.maximum(diff, 0), 0.0).astype(f)
    return {
        "c_onehot": onehot, "c_mask": mask,
        "c_cos": np.concatenate([cos, cos]), "c_sin": np.concatenate([sin, -sin]),
        "c_decay": decay, "c_ident": np.eye(P, dtype=f),
    }


def hybrid_block(nc, x, p, g_mix, w_in, w_a, w_b, w_out, g_ple, w_ple_gate, w_ple_proj, rel_bias,
                 g_final, c_onehot, c_mask, c_cos, c_sin, c_decay, c_ident, out):
    x2d = x.rearrange("b s d -> (b s) d")
    p2d = p.rearrange("l b s d -> (l b s) d")
    out2d = out.rearrange("b s d -> (b s) d")
    W_in = w_in.rearrange("l k n -> (l k) n")
    W_a = w_a.rearrange("l k n -> (l k) n")
    W_b = w_b.rearrange("l k n -> (l k) n")
    W_out = w_out.rearrange("l k n -> (l k) n")
    W_pg = w_ple_gate.rearrange("l k n -> (l k) n")
    W_pp = w_ple_proj.rearrange("l k n -> (l k) n")

    bias_row = nc.dram_tensor("bias_row", [NH, REV], F32)
    bias_rep = nc.dram_tensor("bias_rep", [NH * P * REV + REV], F32)

    ple_kept = nc.dram_tensor("ple_kept", [S, D], F32)

    top = [(nc.sbuf_base + 31) // 32 * 32]

    def at(name, shape, dt, offset):
        return nc.alloc_sbuf_tensor_at(name, shape, dt, offset=offset)

    def place(name, shape, dt=F32):
        offset = top[0]
        top[0] += (4 * int(np.prod(shape[1:])) + 31) // 32 * 32
        assert top[0] <= nc.sbuf_usable_end, (name, top[0])
        return at(name, shape, dt, offset), offset

    hT_hi, hT_at = place("hT_hi", [P, KT, S], F32R)
    hT_lo, _ = place("hT_lo", [P, KT, S], F32R)
    yT_hi, yT_at = place("yT_hi", [P, KT, S], F32R)
    yT_lo, _ = place("yT_lo", [P, KT, S], F32R)
    raw, _ = place("raw", [P, RAW, CH])
    w_hi, _ = place("w_hi", [P, SPLIT, CH], F32R)
    w_lo, _ = place("w_lo", [P, SPLIT, CH], F32R)
    pT_hi, _ = place("pT_hi", [P, 2, S], F32R)
    pT_lo, _ = place("pT_lo", [P, 2, S], F32R)
    ident, _ = place("ident", [P, P])
    ones, _ = place("ones", [P, P], F32R)
    gmix_col, _ = place("gmix_col", [P, KT])
    gple_col, _ = place("gple_col", [P, KT])
    eps_col, _ = place("eps_col", [P, 1])
    sq_x, _ = place("sq_x", [P, TT])
    rms_x, _ = place("rms_x", [P, TT])
    inv_x, _ = place("inv_x", [P, TT])
    sq1, _ = place("sq1", [P, TT, NC_])
    sum1, _ = place("sum1", [P, TT])
    rms1, _ = place("rms1", [P, TT])
    inv1, _ = place("inv1", [P, TT])
    half1, _ = place("half1", [P, TT])
    sq2, _ = place("sq2", [P, TT, NC_])
    sum2, _ = place("sum2", [P, TT])
    rms2, _ = place("rms2", [P, TT])
    inv2, _ = place("inv2", [P, TT])
    warm, _ = place("warm", [P, 2])
    k_sum, _ = place("k_sum", [P, 1])
    k_mean, _ = place("k_mean", [P, 1])
    finite, _ = place("finite", [P, 2])
    cap, _ = place("cap", [P, 2])
    neg_max, _ = place("neg_max", [P, TT])
    row_sum, _ = place("row_sum", [P, TT])
    row_inv, _ = place("row_inv", [P, TT])
    region = top[0]
    KIB = 1024
    assert region + 52 * KIB <= nc.sbuf_usable_end
    x_nat = at("x_nat", [P, TT, D], F32, region)
    p_nat = at("p_nat", [P, TT, D_PLE], F32, yT_at)
    onehot = at("onehot", [BUCKETS, REV], F32, yT_at + 4 * KIB)
    mask_row = at("mask_row", [NH, REV], F32, yT_at + 7 * KIB)
    bias_vec = at("bias_vec", [NH, REV], F32, yT_at + 10 * KIB)
    rel_sb = at("rel_sb", [BUCKETS, NH], F32, yT_at + 13 * KIB)
    q_sb = at("q_sb", [P, S], F32, region)
    k_sb = at("k_sb", [P, S], F32, region + 2 * KIB)
    v_sb = at("v_sb", [P, S], F32, region + 4 * KIB)
    z_half = at("z_half", [P, S], F32, region + 6 * KIB)
    z_tanh = at("z_tanh", [P, S], F32, region + 8 * KIB)
    probs = at("probs", [P, 10 * P], F32, region + 10 * KIB)
    v_last = at("v_last", [P, DH], F32, region + 15 * KIB)
    pT_last = at("pT_last", [P, P], F32, region + 15 * KIB + 512)
    probsT_hi = at("probsT_hi", [P, TT, S], F32R, region + 16 * KIB)
    probsT_lo = at("probsT_lo", [P, TT, S], F32R, region + 24 * KIB)
    q_hi = at("q_hi", [P, S], F32R, region + 32 * KIB)
    q_lo = at("q_lo", [P, S], F32R, region + 34 * KIB)
    k_hi = at("k_hi", [P, S], F32R, region + 36 * KIB)
    k_lo = at("k_lo", [P, S], F32R, region + 38 * KIB)
    v_hi = at("v_hi", [P, TT, DH], F32R, region + 40 * KIB)
    v_lo = at("v_lo", [P, TT, DH], F32R, region + 42 * KIB)
    table = at("table", [P, S], F32, region + 44 * KIB)
    y32 = at("y32", [P, S], F32, region + 46 * KIB)
    cos_sb = at("cos_sb", [P, S], F32, region + 48 * KIB)
    sin_sb = at("sin_sb", [P, S], F32, region + 50 * KIB)
    rot_cos = at("rot_cos", [P, S], F32, region + 16 * KIB)
    rot_sin = at("rot_sin", [P, S], F32, region + 18 * KIB)
    o_rms = at("o_rms", [P, S], F32, region + 20 * KIB)
    probs_hi = at("probs_hi", [P, 10 * P], F32R, region + 22 * KIB)
    probs_lo = at("probs_lo", [P, 10 * P], F32R, region + 27 * KIB)
    o_sq = at("o_sq", [P, S], F32, region + 38 * KIB)
    osq_hi = at("osq_hi", [P, S], F32R, region + 32 * KIB)
    osq_lo = at("osq_lo", [P, S], F32R, region + 34 * KIB)
    sq_junk = at("sq_junk", [P, D], F32, yT_at + 16 * KIB)
    ple_out = at("ple_out", [P, TT, D], F32, yT_at + 32 * KIB)
    merged = at("merged", [P, KT, S], F32, region)
    g_tanh = at("g_tanh", [P, 4, S], F32, region + 32 * KIB)
    x_res = at("x_res", [P, TT, D], F32, region)
    junk = at("junk", [P, CH], F32, region + 32 * KIB)
    pg_tanh = at("pg_tanh", [P, TT, CH], F32, region + 32 * KIB)
    ple = at("ple", [P, TT, D], F32, hT_at)
    gfin = at("gfin", [P, D], F32, hT_at + 32 * KIB)
    junk2 = at("junk2", [P, CH], F32, hT_at + 40 * KIB)

    with ExitStack() as ctx:
        bank = [ctx.enter_context(nc.psum_tensor(f"bank{i}", [P, CH], F32)) for i in range(8)]

        def sem(name):
            return ctx.enter_context(nc.semaphore(name))

        ident_landed = sem("ident_landed")
        p_landed = [sem(f"p_landed{c}") for c in range(KP)]
        x_landed = [sem(f"x_landed{t}") for t in range(TT)]
        small_landed, rel_landed = sem("small_landed"), sem("rel_landed")
        sq_done, rms_done, inv_done, scaled = sem("sq_done"), sem("rms_done"), sem("inv_done"), sem("scaled")
        ones_set = sem("ones_set")
        bias_mm, bias_added = sem("bias_mm"), sem("bias_added")
        bias_stored, bias_spread = sem("bias_stored"), sem("bias_spread")
        p_turned, p_hi, p_lo = sem("p_turned"), sem("p_hi"), sem("p_lo")
        x_turned, h_hi, h_lo = sem("x_turned"), sem("h_hi"), sem("h_lo")
        raw_landed = [sem(f"raw_landed{i}") for i in range(RAW)]
        hi_ready, lo_ready, step_done = sem("hi_ready"), sem("lo_ready"), sem("step_done")
        acc_done = sem("acc_done")
        bank_read = [sem(f"bank_read{j}") for j in range(4)]
        merge_read = [sem(f"merge_read{j}") for j in range(4)]
        v_turned, v_hi_ready, v_lo_ready = sem("v_turned"), sem("v_hi_ready"), sem("v_lo_ready")
        qk_hi, qk_lo = sem("qk_hi"), sem("qk_lo")
        w_hi_ready, w_lo_ready = sem("w_hi_ready"), sem("w_lo_ready")
        k_summed, k_mean_ready = sem("k_summed"), sem("k_mean_ready")
        scores_done, gate_finite, cap_ready = sem("scores_done"), sem("gate_finite"), sem("cap_ready")
        biased, max_ready, exp_done = sem("biased"), sem("max_ready"), sem("exp_done")
        inv_ready, probs_ready = sem("inv_ready"), sem("probs_ready")
        p_turn, pT_hi_ready, pT_lo_ready = sem("p_turn"), sem("pT_hi_ready"), sem("pT_lo_ready")
        zs_ready, table_landed, rot_landed = sem("zs_ready"), sem("table_landed"), sem("rot_landed")
        rot_cos_done, rot_sin_done, rotated = sem("rot_cos_done"), sem("rot_sin_done"), sem("rotated")
        pv_done, osq_ready, mean_done, root_ready = sem("pv_done"), sem("osq_ready"), sem("mean_done"), sem("root_ready")
        osq_split = sem("osq_split")
        oinv_ready, gated, y_ready, y_hi, y_lo = sem("oinv_ready"), sem("gated"), sem("y_ready"), sem("y_hi"), sem("y_lo")
        merged_ready, tanh_ready = sem("merged_ready"), sem("tanh_ready")
        m_hi, m_lo = sem("m_hi"), sem("m_lo")
        xres_landed, x1_sq = sem("xres_landed"), sem("x1_sq")
        ple_stored, ple_landed = sem("ple_stored"), sem("ple_landed")
        x1_turned, hp_hi, hp_lo = sem("x1_turned"), sem("hp_hi"), sem("hp_lo")
        sum1_ready, rms1_ready = sem("sum1_ready"), sem("rms1_ready")
        inv1_ready, half1_ready = sem("inv1_ready"), sem("half1_ready")
        gfin_landed, pg_added, x2_ready, x2_sq = sem("gfin_landed"), sem("pg_added"), sem("x2_ready"), sem("x2_sq")
        x2_scaled = sem("x2_scaled")
        sum2_ready, rms2_ready, inv2_ready = sem("sum2_ready"), sem("rms2_ready"), sem("inv2_ready")
        out_ready, last_ready, out_stored = sem("out_ready"), sem("last_ready"), sem("out_stored")

        block = ctx.enter_context(nc.Block())

        def wait_sums(eng, j, group, last_step):
            if j < 3:
                eng.wait_ge(acc_done, group * 3 + (j + 1))
            else:
                eng.wait_ge(step_done, last_step + 1)

        def wait_last_sums(eng, t):
            if t % 2 == 0:
                eng.wait_ge(acc_done, 3 * (G_GATE + NC_ - 1) + t // 2 + 1)
            else:
                eng.wait_ge(step_done, LAST0 + (t // 2 + 1) * KT)

        G_HEAD = NC_
        G_MERGE = G_HEAD + 2 * NH
        G_OUT = G_MERGE + 4 * NC_
        G_GATE = G_OUT + NC_
        R_HEAD = NC_
        R_MERGE = R_HEAD + 2 * NH
        R_OUT = R_MERGE + 2 * NC_
        R_GATE = R_OUT + NC_

        def score_at(t):
            return P * (t * (t + 1) // 2)

        def decayed_at(t):
            return P * (t * TT - t * (t - 1) // 2)

        @block.sync
        def _(sp):
            sp.dma_start(ident[:, :], c_ident).then_inc(ident_landed, 16)
            def vectors():
                with nc.allow_non_contiguous_dma(reason="two [2048] vectors, once"):
                    sp.dma_start(gmix_col[:, :], g_mix.rearrange("l (c p) -> p (l c)", p=P)).then_inc(small_landed, 16)
                    sp.dma_start(gple_col[:, :], g_ple.rearrange("l (c p) -> p (l c)", p=P)).then_inc(small_landed, 16)
                sp.dma_start(rel_sb[:, :], rel_bias).then_inc(rel_landed, 16)
                sp.dma_start(onehot[:, :], c_onehot).then_inc(rel_landed, 16)
                sp.dma_start(mask_row[:, :], c_mask).then_inc(rel_landed, 16)

            def load(step_mod, step, src, waits=True, pairs=False):
                slot = step_mod % RAW
                if waits:
                    sp.wait_ge(lo_ready, step - (RAW - 1))
                dst = raw[:, slot, :].rearrange("p (t c) -> p t c", c=src.shape[-1])
                if pairs:
                    src = src.rearrange("(c two) t n -> two c (t n)", two=2)
                    dst = raw[:, slot, :]
                sp.dma_start(dst, src).then_inc(raw_landed[slot], 16)

            def head_weights(k, family, h):
                cols = W_in[k * P:(k + 1) * P, family * 4 * D_A:(family + 1) * 4 * D_A]
                return cols.rearrange("p (t c) -> p t c", t=4)[:, :, bass.ds(h * DH, DH)]

            def weights(W, k, n):
                return W[k * P:(k + 1) * P, bass.ds(n * CH, CH)].rearrange("p (t c) -> p t c", t=1)

            for n in range(NC_):
                for k in range(KP):
                    if n == 0:
                        sp.dma_start(p_nat[:, :, k * P:(k + 1) * P],
                                     p2d[:, k * P:(k + 1) * P].rearrange("(t p) d -> p t d", p=P)).then_inc(p_landed[k], 16)
                    load(KP * n + k, KP * n + k, weights(W_pp, k, n), waits=False)
            for t in range(TT):
                sp.dma_start(x_nat[:, t, :], x2d[t * P:(t + 1) * P, :]).then_inc(x_landed[t], 16)
            vectors()
            for k in range(KT):
                load(k, HEAD0 + k, head_weights(k, 0, 0))
            sp.wait_ge(bias_added, 2)
            sp.dma_start(bias_row[:, :], bias_vec[:, :]).then_inc(bias_stored, 16)
            sp.wait_ge(bias_stored, 16)
            sp.dma_start(bias_rep[0:NH * P * REV].rearrange("(h i r) -> h i r", h=NH, i=P),
                         bias_row[:, :].rearrange("h (i r) -> h i r", i=1).to_broadcast([NH, P, REV])
                         ).then_inc(bias_spread, 16)

            def bias_table(h):
                first = bias_rep[bass.ds(h * (P * REV) + (P - 1), P * (REV - 1))]
                return first.rearrange("(i r) -> i r", r=REV - 1)[:, 0:S]

            with sp.Fori(1, NH) as h:
                for k in range(KT):
                    load(k, h * KT + (HEAD0 + k), head_weights(k, 0, h))
                    if k == 2:
                        sp.wait_ge(x_turned, KT)
                        sp.wait_ge(bias_spread, 16)
                        sp.dma_start(table[:, :], bias_table(h - 1)).then_inc(table_landed, 16)
            for k in range(KT):
                load(k, HEAD0 + NH * KT + k, head_weights(k, 1, 0))
                if k == 0:
                    sp.wait_ge(probs_ready, TT * (NH - 1))
                    sp.dma_start(table[:, :], bias_table(NH - 1)).then_inc(table_landed, 16)
                    sp.dma_start(cos_sb[:, :], c_cos).then_inc(rot_landed, 16)
                    sp.dma_start(sin_sb[:, :], c_sin).then_inc(rot_landed, 16)
            with sp.Fori(1, NH) as h:
                for k in range(KT):
                    load(k, h * KT + (HEAD0 + NH * KT + k), head_weights(k, 1, h))
                    if k == 0:
                        sp.wait_ge(probs_ready, h * TT + TT * (NH - 1))
                        sp.dma_start(table[:, :], c_decay[bass.ds(h - 1, 1), :, :].rearrange("h p c -> (h p) c")
                                     ).then_inc(table_landed, 16)

            def merge_loads(n, base, last_table):
                for k in range(KT):
                    ahead = 1 if k == KT - 1 else 0
                    sp.wait_ge(lo_ready, base + (k + ahead - (RAW - 1)))
                    load(k, base + k, weights(W_in[:, GATES:GATES + D], k, n), waits=False)
                    if last_table and k == 0:
                        sp.wait_ge(probs_ready, TT * (2 * NH - 1))
                        sp.dma_start(table[:, :], c_decay[NH - 1]).then_inc(table_landed, 16)
                for k in range(KY):
                    load(k, base + (KT + k), weights(W_a, k, n), waits=k > 0)
                for k in range(KT):
                    load(k, base + (KT + KY + k), weights(W_in[:, GATES + D:GATES + 2 * D], k, n))
                for k in range(KY):
                    load(k, base + (2 * KT + KY + k), weights(W_b, k, n), pairs=True)

            merge_loads(0, MERGE0, True)
            with sp.Fori(1, NC_) as n:
                merge_loads(n, n * MERGE_STEPS + MERGE0, False)
            with sp.Fori(0, NC_) as n:
                for k in range(KT):
                    load(k, n * KT + (OUT0 + k), weights(W_out, k, n))
            for k in range(KT):
                load(k, GATE0 + k, weights(W_pg, k, 0))
            sp.wait_ge(step_done, GATE0)
            sp.wait_ge(ple_stored, 16 * NC_)
            for t in range(TT):
                sp.dma_start(ple[:, t, :], ple_kept[t * P:(t + 1) * P, :]).then_inc(ple_landed, 16)
            sp.dma_start(gfin[:, :], g_final.rearrange("(o d) -> o d", o=1).to_broadcast([P, D])
                         ).then_inc(gfin_landed, 16)
            with sp.Fori(1, NC_ - 1) as n:
                for k in range(KT):
                    load(k, n * KT + (GATE0 + k), weights(W_pg, k, n))
            for half in range(2):
                for k in range(KT):
                    load(k, LAST0 + half * KT + k, weights(W_pg, k, NC_ - 1))
            for t in range(TT):
                own = D - CH if t < 2 else D - 2 * CH
                ready = t + 1 if t < 2 else 2 * t
                for of_act in ((True, False) if t < 2 else (False, True)):
                    if of_act:
                        sp.wait_ge(out_ready, t + 1)
                    else:
                        sp.wait_ge(last_ready, ready)
                    part = slice(0, own) if of_act else slice(own, D)
                    sp.dma_start(out2d[t * P:(t + 1) * P, part], x_res[:, t, part]).then_inc(out_stored, 16)
            sp.wait_ge(out_stored, 2 * 16 * TT)

        @block.tensor
        def _(pe):
            def passes(acc, st_hi, st_lo, mv_hi, mv_lo, first, last):
                pe.matmul(acc, st_hi, mv_hi, start=first, stop=False)
                pe.matmul(acc, st_hi, mv_lo, start=False, stop=False)
                return pe.matmul(acc, st_lo, mv_hi, start=False, stop=last)

            def parts_ready(step):
                pe.wait_ge(hi_ready, step + 1)
                pe.wait_ge(lo_ready, step + 1)

            def transposed_step(step_mod, step, accs, a_hi, a_lo, first, last, free=None):
                slot = step_mod % SPLIT
                parts_ready(step)
                for j in range(4):
                    if first and free is not None:
                        free(j)
                    hi, lo = w_hi[:, slot, j * P:(j + 1) * P], w_lo[:, slot, j * P:(j + 1) * P]
                    mm = passes(accs[j][:, :], hi, lo, a_hi, a_lo, first, last)
                    if last and j < 3:
                        mm.then_inc(acc_done, 1)
                mm.then_inc(step_done, 1)

            def natural_step(step_mod, step, accs, a_hi, a_lo, first, last, free=None, tiles=range(TT)):
                slot = step_mod % SPLIT
                parts_ready(step)
                for t in tiles:
                    if first and free is not None:
                        free(t)
                    mm = passes(accs[t][:, :], a_hi[:, t * P:(t + 1) * P], a_lo[:, t * P:(t + 1) * P],
                                w_hi[:, slot, :], w_lo[:, slot, :], first, last)
                    if last and t != tiles[-1]:
                        mm.then_inc(acc_done, 1)
                mm.then_inc(step_done, 1)

            low, high = bank[0:4], bank[4:8]

            pe.wait_ge(ident_landed, 16)
            for c in range(KP):
                pe.wait_ge(p_landed[c], 16)
                for t in range(TT):
                    mm = pe.transpose(bank[6 + c][:, t * P:(t + 1) * P], p_nat[:, t, c * P:(c + 1) * P], ident[:, :])
                mm.then_inc(p_turned, 1)
            for n in range(NC_):
                for k in range(KP):
                    if n == 0:
                        pe.wait_ge(p_hi, k + 1)
                        pe.wait_ge(p_lo, k + 1)
                    step = n * KP + k
                    natural_step(step, step, high if n % 2 else low, pT_hi[:, k, :], pT_lo[:, k, :], k == 0,
                                 k == KP - 1, lambda t: pe.wait_ge(bank_read[t], n - 1) if n > 1 else None)
            pe.wait_ge(rel_landed, 48)
            for i in range(2):
                half = slice(i * REV // 2, (i + 1) * REV // 2)
                pe.wait_ge(bank_read[i], NC_ - 1)
                pe.matmul(bank[i][0:NH, 0:REV // 2], rel_sb[:, :], onehot[:, half],
                          start=True, stop=True).then_inc(bias_mm, 1)

            def turn_x(c):
                if c >= 4:
                    pe.wait_ge(h_lo, c - 3)
                else:
                    pe.wait_ge(bank_read[c], NC_)
                for t in range(TT):
                    if c == 0:
                        pe.wait_ge(scaled, t + 1)
                    mm = pe.transpose(high[c % 4][:, t * P:(t + 1) * P], x_nat[:, t, c * P:(c + 1) * P], ident[:, :])
                mm.then_inc(x_turned, 1)

            def values_turned(J):
                pe.wait_ge(bank_read[2], J + (R_HEAD + 1))
                for t in range(TT):
                    mm = pe.transpose(high[3][:, t * P:(t + 1) * P], v_sb[:, t * P:(t + 1) * P], ident[:, :])
                mm.then_inc(v_turned, 1)

            def attention(k, J):
                if k == 0:
                    pe.wait_ge(y_ready, J + 1)
                    values_turned(J)
                if k == 1:
                    pe.wait_ge(bank_read[0], J + (R_HEAD + 1))
                    pe.wait_ge(bank_read[1], J + (R_HEAD + 1))
                    pe.wait_ge(k_mean_ready, J + 1)
                    for i in range(2):
                        pe.matmul(high[0][:, CH - 2 + i:CH - 1 + i], q_sb[:, (2 + i) * P:(3 + i) * P], k_mean[:, :],
                                  start=True, stop=True)
                    pe.matmul(high[0][:, 0:P], q_sb[:, 0:P], k_sb[:, 0:P], start=True, stop=True
                              ).then_inc(scores_done, 1)
                if k == 2:
                    pe.wait_ge(qk_hi, J * 2 + 2)
                    pe.wait_ge(qk_lo, J * 2 + 2)
                    for t in (1, 2):
                        tile = slice(t * P, (t + 1) * P)
                        passes(high[t][:, 0:(t + 1) * P], q_hi[:, tile], q_lo[:, tile],
                               k_hi[:, 0:(t + 1) * P], k_lo[:, 0:(t + 1) * P], True, True).then_inc(scores_done, 1)
                if k == 3:
                    pe.wait_ge(v_lo_ready, J * 2 + 2)
                    passes(high[3][:, :], q_hi[:, 3 * P:], q_lo[:, 3 * P:], k_hi[:, :], k_lo[:, :], True, True
                           ).then_inc(scores_done, 1)
                for t, at_k in enumerate((8, 9, 10, 11)):
                    if k == at_k:
                        pe.wait_ge(probs_ready, J * TT + (t + 1))
                        for kt in range(t + 1):
                            a = score_at(t) + kt * P
                            mm = pe.transpose(high[t][:, kt * P:(kt + 1) * P], probs[:, a:a + P], ident[:, :])
                        mm.then_inc(p_turn, 1)
                if k == 13:
                    pe.wait_ge(v_hi_ready, J + 1)
                    pe.wait_ge(pT_hi_ready, J * TT + TT)
                    pe.wait_ge(pT_lo_ready, J * (TT + 1) + (TT + 1))
                    for kt in range(TT - 1):
                        passes(high[0][:, kt * P:], v_hi[:, kt, :], v_lo[:, kt, :],
                               probsT_hi[:, kt, kt * P:], probsT_lo[:, kt, kt * P:], kt == 0, False)
                    pe.matmul(high[0][:, (TT - 1) * P:], v_last[:, :], pT_last[:, :], start=False, stop=True
                              ).then_inc(pv_done, 1)

            def retention(k, J):
                if k == 0:
                    pe.wait_ge(y_ready, J + 1)
                    values_turned(J)
                if k == 4:
                    pe.wait_ge(rotated, (J - NH) * 2 + 3)
                    pe.wait_ge(qk_hi, J * 2 + 2)
                    pe.wait_ge(qk_lo, J * 2 + 2)
                    pe.wait_ge(v_lo_ready, J * 2 + 2)
                    for kt in range(TT - 1):
                        tile = slice(kt * P, (kt + 1) * P)
                        passes(high[kt][:, 0:S - kt * P], k_hi[:, tile], k_lo[:, tile],
                               q_hi[:, kt * P:], q_lo[:, kt * P:], True, True).then_inc(scores_done, 1)
                    pe.matmul(high[3][:, 0:P], k_sb[:, 3 * P:], q_sb[:, 3 * P:], start=True, stop=True
                              ).then_inc(scores_done, 1)
                if k == 9:
                    pe.wait_ge(v_hi_ready, J + 1)
                    pe.wait_ge(probs_ready, J * TT + TT)
                    pe.wait_ge(w_hi_ready, (J - NH) * 2 + 2)
                    pe.wait_ge(w_lo_ready, (J - NH) * 2 + 2)
                    for kt in range(TT - 1):
                        a = decayed_at(kt)
                        passes(high[0][:, kt * P:], v_hi[:, kt, :], v_lo[:, kt, :],
                               probs_hi[:, a:a + S - kt * P], probs_lo[:, a:a + S - kt * P], kt == 0, False)
                    pe.matmul(high[0][:, (TT - 1) * P:], v_last[:, :], probs[:, decayed_at(TT - 1):], start=False,
                              stop=True).then_inc(pv_done, 1)
                if k == 11:
                    pe.wait_ge(osq_ready, (J - NH) * 2 + 2)
                    pe.wait_ge(osq_split, J - NH + 1)
                    pe.matmul(high[1][:, :], ones[:, :], osq_hi[:, :], start=True, stop=False)
                    pe.matmul(high[1][:, :], ones[:, :], osq_lo[:, :], start=False, stop=True).then_inc(mean_done, 1)

            def head_group(G, job):
                def free(j):
                    pe.wait_ge(bank_read[j], G + R_HEAD)
                for k in range(KT):
                    if isinstance(G, int) and G == 0:
                        if k == 0:
                            pe.wait_ge(bias_added, 2)
                        pe.wait_ge(h_hi, k + 1)
                        pe.wait_ge(h_lo, k + 1)
                    transposed_step(k, G * KT + (HEAD0 + k), low, hT_hi[:, k, :], hT_lo[:, k, :], k == 0, k == KT - 1,
                                         free)
                    job(k)

            for c in range(4):
                turn_x(c)
            head_group(0, lambda k: turn_x(k + 4) if k + 4 < KT else None)
            with pe.Fori(1, NH) as h:
                head_group(h, lambda k: attention(k, h - 1))
            head_group(NH, lambda k: attention(k, NH - 1))
            with pe.Fori(NH + 1, 2 * NH) as G:
                head_group(G, lambda k: retention(k, G - 1))

            def merge_group(n, base, job):
                def free_low(g):
                    return lambda j: pe.wait_ge(bank_read[j], g)

                def free_high(g, always):
                    return lambda j: pe.wait_ge(merge_read[j], g) if always else None
                for k in range(KT):
                    transposed_step(k, base + k, low, hT_hi[:, k, :], hT_lo[:, k, :], k == 0, k == KT - 1,
                                         free_low(2 * n + R_MERGE))
                    job(k)
                first_chunk = isinstance(n, int) and n == 0
                for k in range(KY):
                    if first_chunk and k == 0:
                        pe.wait_ge(y_hi, NH)
                        pe.wait_ge(y_lo, NH)
                        pe.wait_ge(y_ready, 2 * NH + 1)
                    transposed_step(k, base + (KT + k), high, yT_hi[:, k, :], yT_lo[:, k, :], k == 0, k == KY - 1,
                                         free_high(2 * n, not first_chunk))
                for k in range(KT):
                    transposed_step(k, base + (KT + KY + k), low, hT_hi[:, k, :], hT_lo[:, k, :], k == 0,
                                         k == KT - 1, free_low(2 * n + (R_MERGE + 1)))
                for k in range(KY):
                    if first_chunk and k == 0:
                        pe.wait_ge(y_hi, 2 * NH)
                        pe.wait_ge(y_lo, 2 * NH)
                    transposed_step(k, base + (2 * KT + KY + k), high, yT_hi[:, KY + k, :], yT_lo[:, KY + k, :],
                                         k == 0, k == KY - 1, free_high(2 * n + 1, True))

            merge_group(0, MERGE0, lambda k: retention(k, 2 * NH - 1))
            with pe.Fori(1, NC_) as n:
                merge_group(n, n * MERGE_STEPS + MERGE0, lambda k: None)

            def turn_x1(n, i):
                for t in range(TT):
                    pe.wait_ge(bank_read[t], R_OUT + n + 1)
                if n == 0:
                    pe.wait_ge(merge_read[i], 2 * NC_)
                else:
                    pe.wait_ge(hp_lo, n * 4 + (i - 3))
                for t in range(TT):
                    mm = pe.transpose(high[i][:, t * P:(t + 1) * P],
                                      x_res[:, t, n * CH + i * P:n * CH + (i + 1) * P], ident[:, :])
                mm.then_inc(x1_turned, 1)

            def out_chunk(n, job):
                def free(t):
                    pe.wait_ge(bank_read[t], R_OUT + n)
                for k in range(KT):
                    if isinstance(n, int) and n == 0:
                        pe.wait_ge(m_hi, k + 1)
                        pe.wait_ge(m_lo, k + 1)
                    natural_step(k, n * KT + (OUT0 + k), low, hT_hi[:, k, :], hT_lo[:, k, :],
                                      k == 0, k == KT - 1, free)
                    job(k)

            out_chunk(0, lambda k: None)
            for n in range(1, NC_):
                out_chunk(n, lambda k: turn_x1(n - 1, (k - 3) // 3) if k in (3, 6, 9, 12) else None)

            def gate_chunk(n):
                def free(t):
                    pe.wait_ge(bank_read[t], n + R_GATE)
                for k in range(KT):
                    if isinstance(n, int) and n == 0:
                        pe.wait_ge(hp_hi, k + 1)
                        pe.wait_ge(hp_lo, k + 1)
                    natural_step(k, n * KT + (GATE0 + k), low, yT_hi[:, k, :], yT_lo[:, k, :],
                                 k == 0, k == KT - 1, free)
                    if isinstance(n, int) and n == 0 and k in (3, 6, 9, 12):
                        turn_x1(NC_ - 1, (k - 3) // 3)

            gate_chunk(0)
            with pe.Fori(1, NC_ - 1) as n:
                gate_chunk(n)
            for half in range(2):
                tiles = (2 * half, 2 * half + 1)
                for k in range(KT - SPLIT * half):
                    natural_step(k, LAST0 + half * KT + k, low, yT_hi[:, k, :], yT_lo[:, k, :], k == 0, k == KT - 1,
                                 lambda t: pe.wait_ge(bank_read[t], NC_ - 1 + R_GATE), tiles)
            for t in tiles:
                for k in range(KT - SPLIT, KT):
                    if t == tiles[0]:
                        parts_ready(LAST0 + KT + k)
                    mm = passes(bank[t][:, :], yT_hi[:, k, t * P:(t + 1) * P], yT_lo[:, k, t * P:(t + 1) * P],
                                w_hi[:, k % SPLIT, :], w_lo[:, k % SPLIT, :], False, k == KT - 1)
                    if t == tiles[-1]:
                        mm.then_inc(step_done, 1)
                if t == tiles[0]:
                    mm.then_inc(acc_done, 1)

        def tile_landed(eng, mod, step):
            use = step // RAW * 16 if isinstance(step, int) else (step - mod) * (16 // RAW)
            eng.wait_ge(raw_landed[mod], use + 16)

        def parts_free(eng, step):
            if not (isinstance(step, int) and step < SPLIT):
                eng.wait_ge(step_done, step - (SPLIT - 1))

        def raw_view(tile, pairs):
            return tile.rearrange("p (j c two) -> p j two c", j=4, two=2) if pairs else tile

        def split_view(tile, pairs):
            return tile.rearrange("p (j two c) -> p j two c", j=4, two=2) if pairs else tile

        @block.scalar
        def _(act):
            def split_hi(mod, step, pairs=False):
                if isinstance(step, int) and step >= STEPS:
                    return
                mod = mod % RAW
                tile_landed(act, mod, step)
                parts_free(act, step)
                act.activation(split_view(w_hi[:, mod % SPLIT, :], pairs), raw_view(raw[:, mod, :], pairs), COPY
                               ).then_inc(hi_ready, 1)

            def x_rms(t):
                act.wait_ge(x_landed[t], 16)
                act.activation(sq_junk[:, :], x_nat[:, t, :], ACT.Square, accum_out=sq_x[:, t:t + 1]).then_inc(sq_done, 1)
                act.wait_ge(sq_done, t + 1)
                act.activation(rms_x[:, t:t + 1], sq_x[:, t:t + 1], ACT.Sqrt, bias=eps_col[:, :], scale=1.0 / D
                               ).then_inc(rms_done, 1)

            for c in range(KP):
                split_hi(c, c)
                act.wait_ge(p_turned, c + 1)
                act.activation(pT_hi[:, c, :], bank[6 + c][:, :], COPY).then_inc(p_hi, 1)
            for k in range(KP, LEAD):
                split_hi(k, k)
            act.wait_ge(ones_set, 2)
            for n in range(NC_):
                for k in range(KP):
                    step = n * KP + k
                    split_hi(step + LEAD, step + LEAD)
                if n == 1:
                    x_rms(1)
                if n == 2:
                    x_rms(3)
                for t in (0, 1):
                    wait_sums(act, t, n, None)
                    act.activation(ple_out[:, t, n * CH:(n + 1) * CH], bank[4 * (n % 2) + t][:, :], COPY, scale=0.5
                                   ).then_inc(bank_read[t], 1)
                if n == 0:
                    x_rms(0)
                if n == 1:
                    x_rms(2)

            def h_part(c):
                act.wait_ge(x_turned, c + 1)
                act.wait_ge(small_landed, 32)
                act.activation(hT_hi[:, c, :], bank[4 + c % 4][:, :], COPY, scale=gmix_col[:, c:c + 1]).then_inc(h_hi, 1)

            def part_hi(src, dst):
                act.activation(dst, src, COPY).then_inc(qk_hi, 1)

            def values_hi(J):
                act.wait_ge(v_turned, J + 1)
                act.activation(v_hi[:, :, :].rearrange("p t d -> p (t d)"), bank[7][:, :], COPY).then_inc(v_hi_ready, 1)

            def attention(k, J):
                if k == 0:
                    act.wait_ge(bank_read[0], J + (R_HEAD + 1))
                    part_hi(q_sb[:, :], q_hi[:, :])
                    act.wait_ge(bank_read[1], J + (R_HEAD + 1))
                    part_hi(k_sb[:, :], k_hi[:, :])
                if k == 1:
                    values_hi(J)
                for t in range(TT):
                    if k == 4 + t:
                        act.wait_ge(max_ready, J * TT + (t + 1))
                        a, n = score_at(t), (t + 1) * P
                        act.activation(probs[:, a:a + n], probs[:, a:a + n], ACT.Exp, bias=neg_max[:, t:t + 1],
                                       accum_out=row_sum[:, t:t + 1]).then_inc(exp_done, 1)
                    if k == 9 + t:
                        act.wait_ge(p_turn, J * TT + (t + 1))
                        act.activation(probsT_hi[:, 0:t + 1, t * P:(t + 1) * P],
                                       bank[4 + t][:, 0:(t + 1) * P].rearrange("p (k q) -> p k q", q=P), COPY
                                       ).then_inc(pT_hi_ready, 1)
                y_part(k, J)

            def y_part(k, J):
                if k == 15:
                    act.wait_ge(y_ready, J + 2)
                    act.activation(yT_hi[:, bass.ds(J, 1), :].rearrange("p j s -> p (j s)"), y32[:, :], COPY).then_inc(y_hi, 1)

            def retention(k, J):
                b = J - NH
                if k == 1:
                    values_hi(J)
                    act.wait_ge(rotated, b * 2 + 2)
                    part_hi(q_sb[:, :], q_hi[:, :])
                if k == 2:
                    act.wait_ge(rotated, b * 2 + 3)
                    part_hi(k_sb[:, :], k_hi[:, :])
                for i in range(2):
                    if k == 6 + i:
                        act.wait_ge(probs_ready, J * TT + (2 * i + 2))
                        cols = slice(decayed_at(2 * i), decayed_at(2 * i + 2))
                        act.activation(probs_hi[:, cols], probs[:, cols], COPY).then_inc(w_hi_ready, 1)
                if k == 10:
                    act.wait_ge(pv_done, J + 1)
                    act.activation(o_sq[:, :], bank[4][:, :], ACT.Square).then_inc(osq_ready, 1)
                    act.activation(osq_hi[:, :], bank[4][:, :], ACT.Square).then_inc(osq_ready, 1)
                if k == 12:
                    act.wait_ge(mean_done, J - (NH - 1))
                    act.activation(o_rms[:, :], bank[5][:, :], ACT.Sqrt, bias=eps_col[:, :]).then_inc(root_ready, 1)
                y_part(k, J)

            def head_group(G, job, pairs, next_pairs):
                first = isinstance(G, int) and G == 0
                for k in range(KT):
                    split_hi(k + LEAD, G * KT + (HEAD0 + k + LEAD), pairs if k + LEAD < KT else next_pairs)
                    job(k)
                wait_sums(act, 0, G + G_HEAD, None)
                if not first:
                    act.wait_ge(scores_done, G * TT)
                act.activation(q_sb[:, :], bank[0][:, :], COPY, scale=float(DH) ** -0.5).then_inc(bank_read[0], 1)
                wait_sums(act, 2, G + G_HEAD, None)
                if not first:
                    act.wait_ge(v_turned, G)
                act.activation(v_sb[:, :], bank[2][:, :], COPY).then_inc(bank_read[2], 1)
                act.wait_ge(bank_read[3], G + (R_HEAD + 1))
                if not first:
                    act.wait_ge(zs_ready, G)
                act.activation(z_tanh[:, :], z_half[:, :], ACT.Tanh).then_inc(tanh_ready, 1)

            for c in range(4):
                h_part(c)
            for n in range(NC_):
                for t in range(TT):
                    act.wait_ge(bank_read[t], n + 1)
                act.dma_start(ple_kept[:, n * CH:(n + 1) * CH].rearrange("(t p) c -> p t c", p=P),
                              ple_out[:, :, n * CH:(n + 1) * CH]).then_inc(ple_stored, 16)
            head_group(0, lambda k: h_part(k + 4) if k + 4 < KT else None, False, False)
            with act.Fori(1, NH - 1) as h:
                head_group(h, lambda k: attention(k, h - 1), False, False)
            head_group(NH - 1, lambda k: attention(k, NH - 2), False, True)
            head_group(NH, lambda k: attention(k, NH - 1), True, True)
            with act.Fori(NH + 1, 2 * NH - 1) as G:
                head_group(G, lambda k: retention(k, G - 1), True, True)
            head_group(2 * NH - 1, lambda k: retention(k, 2 * NH - 2), True, False)

            def merge_group(n, base, job):
                first_chunk = isinstance(n, int) and n == 0
                for k in range(KT):
                    split_hi(k + LEAD, base + (k + LEAD))
                    job(k)
                for j in range(4):
                    wait_sums(act, j, n * 4 + G_MERGE, base + (KT - 1))
                    if not first_chunk:
                        act.wait_ge(merged_ready, n * 4 + (j - 3))
                    act.activation(g_tanh[:, j, :], bank[j][:, :], ACT.Tanh, scale=0.5).then_inc(bank_read[j], 1)
                for k in range(KY + KT):
                    split_hi(k + LEAD, base + (KT + k + LEAD))
                for j in range(4):
                    wait_sums(act, j, n * 4 + (G_MERGE + 2), base + (2 * KT + KY - 1))
                    act.wait_ge(merge_read[j], n * 2 + 1)
                    act.activation(g_tanh[:, j, :], bank[j][:, :], ACT.Tanh, scale=0.5).then_inc(bank_read[j], 1)
                for k in range(KY):
                    split_hi(k + LEAD, base + (2 * KT + KY + k + LEAD))
                if isinstance(n, int) and n == NC_ - 1:
                    for c in range(4):
                        merged_part(c)

            merge_group(0, MERGE0, lambda k: retention(k, 2 * NH - 1))
            def merged_part(c):
                act.wait_ge(merged_ready, c + 1)
                if c == 0:
                    act.wait_ge(step_done, OUT0 - KY)
                act.activation(hT_hi[:, c, :], merged[:, c, :], COPY, scale=0.5).then_inc(m_hi, 1)

            def hp_part(c):
                act.wait_ge(x1_turned, c + 1)
                act.activation(yT_hi[:, c, :], bank[4 + c % 4][:, :], COPY, scale=gple_col[:, c:c + 1]).then_inc(hp_hi, 1)

            def x1_square(n, t):
                act.wait_ge(bank_read[t], R_OUT + n + 1)
                if n or t:
                    act.wait_ge(x1_sq, n * TT + t)
                act.activation(junk[:, :], x_res[:, t, n * CH:(n + 1) * CH], ACT.Square,
                               accum_out=sq1[:, t, n:n + 1]).then_inc(x1_sq, 1)

            with act.Fori(1, NC_ - 1) as n:
                merge_group(n, n * MERGE_STEPS + MERGE0, lambda k: None)
            merge_group(NC_ - 1, (NC_ - 1) * MERGE_STEPS + MERGE0, lambda k: None)
            for n in range(NC_):
                for k in range(KT):
                    split_hi(k + LEAD, OUT0 + n * KT + k + LEAD)
                    if n == 0:
                        for c in (4 + 2 * k, 5 + 2 * k):
                            if c < KT:
                                merged_part(c)
                        if k == 7:
                            act.wait_ge(m_lo, KT)
                            for t in range(TT):
                                act.dma_start(x_res[:, t, :], x2d[t * P:(t + 1) * P, :]).then_inc(xres_landed, 16)
                    else:
                        if k in (0, 1, 2, 3):
                            x1_square(n - 1, k)
                        if k in (4, 7, 10, 13):
                            hp_part((n - 1) * 4 + (k - 4) // 3)

            def x2_square(t, n):
                if t or not (isinstance(n, int) and n == 0):
                    act.wait_ge(x2_sq, n * TT + t)
                act.wait_ge(x2_ready, n * TT + (t + 1))
                act.activation(junk2[:, :], x_res[:, t, bass.ds(n * CH, CH)], ACT.Square,
                               accum_out=sq2[:, t, bass.ds(n, 1)]).then_inc(x2_sq, 1)

            def gate_chunk(n):
                first = isinstance(n, int) and n == 0
                for k in range(KT):
                    split_hi(k + LEAD, n * KT + (GATE0 + k + LEAD))
                    if first:
                        if k in (0, 1, 2, 3):
                            x1_square(NC_ - 1, k)
                        if k in (4, 7, 10, 13):
                            hp_part((NC_ - 1) * 4 + (k - 4) // 3)
                        if k == 6:
                            act.wait_ge(sum1_ready, 1)
                            act.activation(rms1[:, :], sum1[:, :], ACT.Sqrt, bias=eps_col[:, :], scale=1.0 / D
                                           ).then_inc(rms1_ready, 1)
                    elif k in (1, 4, 7, 10):
                        x2_square(k // 3, n - 1)
                for t in range(TT):
                    if first:
                        act.wait_ge(half1_ready, 1)
                    else:
                        act.wait_ge(x2_ready, n * TT + (t - 3))
                    wait_sums(act, t, n + G_GATE, n * KT + (GATE0 + KT - 1))
                    act.activation(pg_tanh[:, t, :], bank[t][:, :], ACT.Tanh, scale=half1[:, t:t + 1]
                                   ).then_inc(bank_read[t], 1)

            gate_chunk(0)
            with act.Fori(1, NC_ - 1) as n:
                gate_chunk(n)
            last = NC_ - 1

            def last_tanh(t):
                act.wait_ge(x2_ready, last * TT + t - 3)
                wait_last_sums(act, t)
                act.activation(pg_tanh[:, t, :], bank[t][:, :], ACT.Tanh, scale=half1[:, t:t + 1]
                               ).then_inc(bank_read[t], 1)

            def last_root(t):
                act.wait_ge(sum2_ready, t + 1)
                act.activation(rms2[:, t:t + 1], sum2[:, t:t + 1], ACT.Sqrt, bias=eps_col[:, :], scale=1.0 / D
                               ).then_inc(rms2_ready, 1)

            def last_scale(t):
                act.wait_ge(inv2_ready, t + 1)
                act.wait_ge(x2_scaled, last * TT)
                chunks = slice(0, (last if t < 2 else last - 1) * CH)
                act.activation(x_res[:, t, chunks], x_res[:, t, chunks], COPY, scale=inv2[:, t:t + 1]
                               ).then_inc(out_ready, 1)

            for k in range(KT):
                split_hi(k + LEAD, LAST0 + k + LEAD)
                if k in (1, 4, 7, 10):
                    x2_square(k // 3, last - 1)
            for k in range(KT):
                split_hi(k + LEAD, LAST0 + KT + k + LEAD)
                if k < 2:
                    last_tanh(k)
                if k in (2, 3):
                    x2_square(k - 2, last)
                if k == 4:
                    last_root(0)
                    last_root(1)
                if k in (7, 9):
                    last_scale((k - 7) // 2)
                if k == 5:
                    act.activation(warm[:, 0:1], eps_col[:, :], ACT.Tanh)
            last_tanh(2)
            x2_square(2, last)
            last_tanh(3)
            act.activation(warm[:, 1:2], eps_col[:, :], ACT.Sqrt)
            last_root(2)
            x2_square(3, last)
            last_scale(2)
            last_root(3)
            last_scale(3)

        @block.vector
        def _(dve):
            def split_lo(mod, step, pairs=False):
                if isinstance(step, int) and step >= STEPS:
                    return
                mod = mod % RAW
                tile_landed(dve, mod, step)
                parts_free(dve, step)
                dve.wait_ge(hi_ready, step + 1)
                dve.tensor_tensor(split_view(w_lo[:, mod % SPLIT, :], pairs), raw_view(raw[:, mod, :], pairs),
                                  split_view(w_hi[:, mod % SPLIT, :].bitcast(F32), pairs),
                                  ALU.subtract).then_inc(lo_ready, 1)

            dve.memset(eps_col[:, :], EPS).then_inc(ones_set, 1)
            dve.memset(ones[:, :].bitcast(F32), 1.0 / P).then_inc(ones_set, 1)
            dve.memset(k_sum[:, :], 0.0).then_inc(y_ready, 1)
            dve.memset(k_mean[:, :], 0.0).then_inc(rotated, 1)
            def x_scale(t):
                dve.wait_ge(rms_done, t + 1)
                dve.reciprocal(inv_x[:, t:t + 1], rms_x[:, t:t + 1]).then_inc(inv_done, 1)
                dve.wait_ge(inv_done, t + 1)
                dve.tensor_scalar(x_nat[:, t, :], x_nat[:, t, :], inv_x[:, t:t + 1], None, ALU.mult).then_inc(scaled, 1)

            for c in range(KP):
                split_lo(c, c)
                dve.wait_ge(p_hi, c + 1)
                dve.tensor_tensor(pT_lo[:, c, :], bank[6 + c][:, :], pT_hi[:, c, :].bitcast(F32), ALU.subtract
                                  ).then_inc(p_lo, 1)
            for k in range(KP, LEAD):
                split_lo(k, k)
            for n in range(NC_):
                for k in range(KP):
                    split_lo(n * KP + k + LEAD, n * KP + k + LEAD)
                if n in (1, 2):
                    x_scale(2 * (n - 1))
                for t in (2, 3):
                    wait_sums(dve, t, n, n * KP + KP - 1)
                    dve.tensor_scalar(ple_out[:, t, n * CH:(n + 1) * CH], bank[4 * (n % 2) + t][:, :], 0.5, None, ALU.mult
                                      ).then_inc(bank_read[t], 1)
                if n in (1, 2):
                    x_scale(2 * n - 1)
            for i in range(2):
                half = slice(i * REV // 2, (i + 1) * REV // 2)
                dve.wait_ge(bias_mm, i + 1)
                dve.tensor_tensor(bias_vec[:, half], bank[i][0:NH, 0:REV // 2], mask_row[:, half], ALU.add
                                  ).then_inc(bias_added, 1)

            def h_part(c):
                dve.wait_ge(h_hi, c + 1)
                dve.scalar_tensor_tensor(out=hT_lo[:, c, :], in0=bank[4 + c % 4][:, :], scalar=gmix_col[:, c:c + 1],
                                         in1=hT_hi[:, c, :].bitcast(F32), op0=ALU.mult, op1=ALU.subtract
                                         ).then_inc(h_lo, 1)

            def silu(J):
                dve.wait_ge(tanh_ready, J + 1)
                dve.scalar_tensor_tensor(out=z_half[:, :], in0=z_tanh[:, :], scalar=1.0, in1=z_half[:, :],
                                         op0=ALU.add, op1=ALU.mult).then_inc(zs_ready, 1)

            def part_lo(J, i, src, hi, dst):
                dve.wait_ge(qk_hi, J * 2 + (i + 1))
                dve.tensor_tensor(dst, src, hi.bitcast(F32), ALU.subtract).then_inc(qk_lo, 1)

            def values_lo(J):
                dve.wait_ge(v_hi_ready, J + 1)
                dve.tensor_tensor(v_lo[:, :, :].rearrange("p t d -> p (t d)"), bank[7][:, :],
                                  v_hi[:, :, :].rearrange("p t d -> p (t d)").bitcast(F32), ALU.subtract
                                  ).then_inc(v_lo_ready, 1)
                dve.tensor_copy(v_last[:, :], bank[7][:, (TT - 1) * P:]).then_inc(v_lo_ready, 1)

            def y_part(k, J):
                if k == 15:
                    dve.wait_ge(y_hi, J + 1)
                    dve.tensor_tensor(yT_lo[:, bass.ds(J, 1), :].rearrange("p j s -> p (j s)"), y32[:, :],
                                      yT_hi[:, bass.ds(J, 1), :].rearrange("p j s -> p (j s)").bitcast(F32),
                                      ALU.subtract).then_inc(y_lo, 1)

            def attention(k, J):
                if k == 0:
                    dve.wait_ge(bank_read[1], J + (R_HEAD + 1))
                    dve.tensor_reduce(k_sum[:, :], k_sb[:, 0:BLOCK], AX.X, ALU.add).then_inc(k_summed, 1)
                    dve.wait_ge(k_summed, J + 1)
                    dve.tensor_scalar(k_mean[:, :], k_sum[:, :], float(DH) ** 0.5 / BLOCK, None, ALU.mult
                                      ).then_inc(k_mean_ready, 1)
                    part_lo(J, 0, q_sb[:, :], q_hi[:, :], q_lo[:, :])
                    part_lo(J, 1, k_sb[:, :], k_hi[:, :], k_lo[:, :])
                if k == 1:
                    silu(J)
                if k == 2:
                    values_lo(J)
                if k == 2:
                    dve.wait_ge(scores_done, J * TT + 1)
                    dve.tensor_scalar(finite[:, :], bank[4][:, CH - 2:CH], 0.0, 0.0, ALU.mult, ALU.is_equal
                                      ).then_inc(gate_finite, 1)
                    dve.wait_ge(gate_finite, J + 1)
                    dve.tensor_scalar(cap[:, :], finite[:, :], 2 * BIG, -BIG, ALU.mult, ALU.add).then_inc(cap_ready, 1)
                for t in range(TT):
                    a, n = score_at(t), (t + 1) * P
                    tab = (TT - 1 - t) * P
                    if k == 3 + t:
                        dve.wait_ge(scores_done, J * TT + (t + 1))
                        dve.wait_ge(table_landed, J * 16 + 16)
                        past = BLOCK if t * P >= BLOCK else 0
                        if past:
                            dve.wait_ge(cap_ready, J + 1)
                            dve.scalar_tensor_tensor(out=probs[:, a:a + past], in0=bank[4 + t][:, 0:past],
                                                     scalar=cap[:, t - 2:t - 1], in1=table[:, tab:tab + past],
                                                     op0=ALU.min, op1=ALU.add).then_inc(biased, 1)
                        dve.tensor_tensor(probs[:, a + past:a + n], bank[4 + t][:, past:n], table[:, tab + past:tab + n],
                                          ALU.add).then_inc(biased, 1)
                        dve.wait_ge(biased, J * 6 + (1, 2, 4, 6)[t])
                        dve.tensor_reduce(neg_max[:, t:t + 1], probs[:, a:a + n], AX.X, ALU.max, negate=True
                                          ).then_inc(max_ready, 1)
                    if k == 5 + t:
                        dve.wait_ge(exp_done, J * TT + (t + 1))
                        dve.reciprocal(row_inv[:, t:t + 1], row_sum[:, t:t + 1]).then_inc(inv_ready, 1)
                        dve.wait_ge(inv_ready, J * TT + (t + 1))
                        dve.tensor_scalar(probs[:, a:a + n], probs[:, a:a + n], row_inv[:, t:t + 1], None, ALU.mult
                                          ).then_inc(probs_ready, 1)
                for t in range(TT):
                    if k == 9 + t:
                        dve.wait_ge(pT_hi_ready, J * TT + (t + 1))
                        tile = slice(t * P, (t + 1) * P)
                        dve.tensor_tensor(probsT_lo[:, 0:t + 1, tile],
                                          bank[4 + t][:, 0:(t + 1) * P].rearrange("p (k q) -> p k q", q=P),
                                          probsT_hi[:, 0:t + 1, tile].bitcast(F32), ALU.subtract
                                          ).then_inc(pT_lo_ready, 1)
                        if t == TT - 1:
                            dve.tensor_copy(pT_last[:, :], bank[7][:, (TT - 1) * P:]).then_inc(pT_lo_ready, 1)
                if k == 14:
                    dve.wait_ge(pv_done, J + 1)
                    dve.tensor_tensor(y32[:, :], bank[4][:, :], z_half[:, :], ALU.mult).then_inc(y_ready, 1)
                y_part(k, J)

            def retention(k, J):
                b = J - NH
                if k == 0:
                    dve.wait_ge(rot_landed, 32)
                if k == 2:
                    part_lo(J, 0, q_sb[:, :], q_hi[:, :], q_lo[:, :])
                    part_lo(J, 1, k_sb[:, :], k_hi[:, :], k_lo[:, :])
                if k == 3:
                    values_lo(J)
                    silu(J)
                for i, src in enumerate((q_sb, k_sb)):
                    if k == i:
                        dve.wait_ge(bank_read[i], J + (R_HEAD + 1))
                        dve.wait_ge(rotated, b * 2 + (i + 1))
                        dve.tensor_tensor(rot_cos[:, :], src[:, :], cos_sb[:, :], ALU.mult).then_inc(rot_cos_done, 1)
                        for lo, hi in ((0, 64), (64, 0)):
                            dve.tensor_tensor(rot_sin[lo:lo + 64, :], src[hi:hi + 64, :], sin_sb[hi:hi + 64, :], ALU.mult
                                              ).then_inc(rot_sin_done, 1)
                        dve.wait_ge(rot_cos_done, b * 2 + (i + 1))
                        dve.wait_ge(rot_sin_done, b * 4 + (2 * i + 2))
                        dve.tensor_tensor(src[:, :], rot_cos[:, :], rot_sin[:, :], ALU.add).then_inc(rotated, 1)
                for kt in range(TT):
                    if k == 5 + kt // 2:
                        a, n = decayed_at(kt), S - kt * P
                        dve.wait_ge(scores_done, J * TT + (kt + 1))
                        dve.wait_ge(table_landed, J * 16 + 16)
                        dve.tensor_tensor(probs[:, a:a + n], bank[4 + kt][:, 0:n], table[:, 0:n], ALU.mult
                                          ).then_inc(probs_ready, 1)
                for i in range(2):
                    if k == 7 + i:
                        dve.wait_ge(w_hi_ready, b * 2 + (i + 1))
                        cols = slice(decayed_at(2 * i), decayed_at(2 * i + 2))
                        dve.tensor_tensor(probs_lo[:, cols], probs[:, cols], probs_hi[:, cols].bitcast(F32), ALU.subtract
                                          ).then_inc(w_lo_ready, 1)
                if k == 10:
                    dve.wait_ge(osq_ready, b * 2 + 2)
                    dve.tensor_tensor(osq_lo[:, :], o_sq[:, :], osq_hi[:, :].bitcast(F32), ALU.subtract
                                      ).then_inc(osq_split, 1)
                if k == 13:
                    dve.wait_ge(root_ready, b + 1)
                    dve.reciprocal(o_rms[:, :], o_rms[:, :]).then_inc(oinv_ready, 1)
                    dve.tensor_tensor(y32[:, :], bank[4][:, :], z_half[:, :], ALU.mult).then_inc(gated, 1)
                    dve.wait_ge(oinv_ready, b + 1)
                    dve.wait_ge(gated, b + 1)
                    dve.tensor_tensor(y32[:, :], y32[:, :], o_rms[:, :], ALU.mult).then_inc(y_ready, 1)
                y_part(k, J)

            def head_group(G, job, pairs, next_pairs):
                first = isinstance(G, int) and G == 0
                for k in range(KT):
                    split_lo(k + LEAD, G * KT + (HEAD0 + k + LEAD), pairs if k + LEAD < KT else next_pairs)
                    job(k)
                wait_sums(dve, 1, G + G_HEAD, None)
                if not first:
                    dve.wait_ge(scores_done, G * TT)
                dve.tensor_copy(k_sb[:, :], bank[1][:, :]).then_inc(bank_read[1], 1)
                wait_sums(dve, 3, G + G_HEAD, G * KT + (HEAD0 + KT - 1))
                dve.tensor_scalar(z_half[:, :], bank[3][:, :], 0.5, None, ALU.mult).then_inc(bank_read[3], 1)

            for c in range(4):
                h_part(c)
            head_group(0, lambda k: h_part(k + 4) if k + 4 < KT else None, False, False)
            dve.wait_ge(ple_stored, 16 * NC_)
            with dve.Fori(1, NH - 1) as h:
                head_group(h, lambda k: attention(k, h - 1), False, False)
            head_group(NH - 1, lambda k: attention(k, NH - 2), False, True)
            head_group(NH, lambda k: attention(k, NH - 1), True, True)
            with dve.Fori(NH + 1, 2 * NH - 1) as G:
                head_group(G, lambda k: retention(k, G - 1), True, True)
            head_group(2 * NH - 1, lambda k: retention(k, 2 * NH - 2), True, False)

            def merge_group(n, base, job):
                for k in range(KT):
                    split_lo(k + LEAD, base + (k + LEAD))
                    job(k)
                for k in range(KY):
                    split_lo(k + LEAD, base + (KT + k + LEAD))
                for j in range(4):
                    wait_sums(dve, j, n * 4 + (G_MERGE + 1), base + (KT + KY - 1))
                    dve.wait_ge(bank_read[j], n * 2 + (R_MERGE + 1))
                    dve.scalar_tensor_tensor(out=merged[:, bass.ds(n * 4 + j, 1), :].rearrange("p j s -> p (j s)"),
                                             in0=g_tanh[:, j, :], scalar=1.0, in1=bank[4 + j][:, :],
                                             op0=ALU.add, op1=ALU.mult).then_inc(merge_read[j], 1)
                for k in range(KT + KY):
                    split_lo(k + LEAD, base + (KT + KY + k + LEAD))
                if isinstance(n, int) and n == NC_ - 1:
                    for c in range(4):
                        merged_part(c)
                for j in range(4):
                    wait_sums(dve, j, n * 4 + (G_MERGE + 3), base + (MERGE_STEPS - 1))
                    dve.wait_ge(bank_read[j], n * 2 + (R_MERGE + 2))
                    dve.scalar_tensor_tensor(out=g_tanh[:, j, :], in0=g_tanh[:, j, :], scalar=1.0,
                                             in1=bank[4 + j][:, :], op0=ALU.add, op1=ALU.mult).then_inc(merge_read[j], 1)
                    dve.wait_ge(merge_read[j], n * 2 + 2)
                    tile = merged[:, bass.ds(n * 4 + j, 1), :].rearrange("p j s -> p (j s)")
                    dve.tensor_tensor(tile, tile, g_tanh[:, j, :], ALU.add).then_inc(merged_ready, 1)

            merge_group(0, MERGE0, lambda k: retention(k, 2 * NH - 1))
            def merged_part(c):
                dve.wait_ge(m_hi, c + 1)
                dve.scalar_tensor_tensor(out=hT_lo[:, c, :], in0=merged[:, c, :], scalar=0.5,
                                         in1=hT_hi[:, c, :].bitcast(F32), op0=ALU.mult, op1=ALU.subtract
                                         ).then_inc(m_lo, 1)

            def hp_part(c):
                dve.wait_ge(hp_hi, c + 1)
                dve.scalar_tensor_tensor(out=yT_lo[:, c, :], in0=bank[4 + c % 4][:, :], scalar=gple_col[:, c:c + 1],
                                         in1=yT_hi[:, c, :].bitcast(F32), op0=ALU.mult, op1=ALU.subtract
                                         ).then_inc(hp_lo, 1)

            with dve.Fori(1, NC_ - 1) as n:
                merge_group(n, n * MERGE_STEPS + MERGE0, lambda k: None)
            merge_group(NC_ - 1, (NC_ - 1) * MERGE_STEPS + MERGE0, lambda k: None)
            for n in range(NC_):
                for k in range(KT):
                    split_lo(k + LEAD, OUT0 + n * KT + k + LEAD)
                    if n == 0:
                        for c in (4 + 2 * k, 5 + 2 * k):
                            if c < KT:
                                merged_part(c)
                    elif k in (4, 7, 10, 13):
                        hp_part((n - 1) * 4 + (k - 4) // 3)
                if n == 0:
                    dve.wait_ge(xres_landed, 16 * TT)
                for t in range(TT):
                    wait_sums(dve, t, G_OUT + n, OUT0 + n * KT + KT - 1)
                    chunk = x_res[:, t, n * CH:(n + 1) * CH]
                    dve.tensor_tensor(chunk, bank[t][:, :], chunk, ALU.add).then_inc(bank_read[t], 1)

            def x2_times_g(t, n):
                dve.wait_ge(x2_sq, n * TT + (t + 1))
                chunk = x_res[:, t, bass.ds(n * CH, CH)]
                dve.tensor_tensor(chunk, chunk, gfin[:, bass.ds(n * CH, CH)], ALU.mult).then_inc(x2_scaled, 1)

            def x2(t, n):
                dve.wait_ge(bank_read[t], n + (R_GATE + 1))
                dve.scalar_tensor_tensor(out=pg_tanh[:, t, :], in0=pg_tanh[:, t, :], scalar=1.0,
                                         in1=ple[:, t, bass.ds(n * CH, CH)], op0=ALU.add, op1=ALU.mult
                                         ).then_inc(pg_added, 1)
                dve.wait_ge(pg_added, n * TT + (t + 1))
                chunk = x_res[:, t, bass.ds(n * CH, CH)]
                dve.tensor_tensor(chunk, chunk, pg_tanh[:, t, :], ALU.add).then_inc(x2_ready, 1)

            def gate_chunk(n):
                first = isinstance(n, int) and n == 0
                for k in range(KT):
                    split_lo(k + LEAD, n * KT + (GATE0 + k + LEAD))
                    if first:
                        if k in (4, 7, 10, 13):
                            hp_part((NC_ - 1) * 4 + (k - 4) // 3)
                        if k == 5:
                            dve.wait_ge(x1_sq, NC_ * TT)
                            dve.tensor_reduce(sum1[:, :], sq1[:, :, :], AX.X, ALU.add).then_inc(sum1_ready, 1)
                        if k == 8:
                            dve.wait_ge(rms1_ready, 1)
                            dve.reciprocal(inv1[:, :], rms1[:, :]).then_inc(inv1_ready, 1)
                            dve.wait_ge(inv1_ready, 1)
                            dve.tensor_scalar(half1[:, :], inv1[:, :], 0.5, None, ALU.mult).then_inc(half1_ready, 1)
                    else:
                        x2_of_chunk(k, n - 1)

            def x2_of_chunk(k, n):
                if k in (0, 3, 6, 9):
                    x2(k // 3, n)
                if k in (2, 5, 8, 11):
                    x2_times_g(k // 3, n)

            gate_chunk(0)
            dve.wait_ge(ple_landed, 16 * TT)
            dve.wait_ge(gfin_landed, 16)
            with dve.Fori(1, NC_ - 1) as n:
                gate_chunk(n)
            last = NC_ - 1

            def last_sum(t):
                dve.wait_ge(x2_sq, last * TT + t + 1)
                dve.tensor_reduce(sum2[:, t:t + 1], sq2[:, t, :], AX.X, ALU.add).then_inc(sum2_ready, 1)

            def last_inv(t):
                dve.wait_ge(rms2_ready, t + 1)
                dve.reciprocal(inv2[:, t:t + 1], rms2[:, t:t + 1]).then_inc(inv2_ready, 1)

            def last_scale(t):
                dve.wait_ge(inv2_ready, t + 1)
                dve.scalar_tensor_tensor(out=x_res[:, t, last * CH:], in0=x_res[:, t, last * CH:], scalar=inv2[:, t:t + 1],
                                         in1=gfin[:, last * CH:], op0=ALU.mult, op1=ALU.mult).then_inc(last_ready, 1)
                if t >= 2:
                    chunk = x_res[:, t, (last - 1) * CH:last * CH]
                    dve.tensor_scalar(chunk, chunk, inv2[:, t:t + 1], None, ALU.mult).then_inc(last_ready, 1)

            for k in range(KT):
                split_lo(k + LEAD, LAST0 + k + LEAD)
                x2_of_chunk(k, last - 1)
            for k in range(KT):
                split_lo(k + LEAD, LAST0 + KT + k + LEAD)
                if k in (1, 2):
                    x2(k - 1, last)
                if k in (3, 4):
                    last_sum(k - 3)
                if k == 5:
                    last_inv(0)
                    last_inv(1)
                if k in (6, 8):
                    last_scale((k - 6) // 2)
            x2(2, last)
            last_sum(2)
            x2(3, last)
            last_inv(2)
            last_scale(2)
            last_sum(3)
            last_inv(3)
            last_scale(3)


INPUTS = ["x", "p", "g_mix", "w_in", "w_a", "w_b", "w_out", "g_ple", "w_ple_gate", "w_ple_proj", "rel_bias",
          "g_final"]


def kernel(**inputs):
    import concourse.bacc as bacc
    from concourse.bass_utils import run_bass_kernel_spmd

    nc = bacc.Bacc("TRN2", target_bir_lowering=False, num_devices=1, dynamic_dma_scratch_size=2048)
    given = {name: np.ascontiguousarray(inputs[name]) for name in INPUTS}
    given.update(shape_constants())
    arrays, args = {}, {}
    for name, a in given.items():
        arrays[f"in_{name}"] = a
        args[name] = nc.dram_tensor(f"in_{name}", a.shape, mybir.dt.from_np(a.dtype), kind="ExternalInput").ap()
    out = nc.dram_tensor("out", inputs["x"].shape, F32, kind="ExternalOutput").ap()
    hybrid_block(nc, out=out, **args)
    result = run_bass_kernel_spmd(nc, [arrays], core_ids=[0])
    return result.results[0]["out"]
```
